# Optimizing a Trainium2 kernel written in Bass

```python
import math
import jax, jax.numpy as jnp
from jax import lax
import numpy as np

D_MODEL = 2048
BATCH = 1
SEQ = 512
DEPTH = 1

MIX_WIDTH = D_MODEL
ATTN_WIDTH = MIX_WIDTH // 2
LRU_WIDTH = MIX_WIDTH - ATTN_WIDTH
HEAD_DIM = 128
N_ATTN_HEADS = ATTN_WIDTH // HEAD_DIM
N_LRU_BLOCKS = 8
LRU_BLOCK = LRU_WIDTH // N_LRU_BLOCKS
CONV_WIDTH = 4
LRU_C = 8.0
Q_BLOCK = 128
D_FF = -(-8 * D_MODEL // (3 * 256)) * 256
IN_WIDTH = 3 * ATTN_WIDTH + 2 * LRU_WIDTH
RMS_EPS = 1e-6

kernel_name = "hymba_stickbreak_rglru_swiglu_sandwich"

def rmsnorm(x, gain):
    xf = x.astype(jnp.float32)
    var = jnp.mean(xf * xf, axis=-1, keepdims=True)
    return (xf * lax.rsqrt(var + RMS_EPS)).astype(x.dtype) * gain

def stick_breaking_attention(q, k, v):
    b, h, s, dh = q.shape
    n_blk = s // Q_BLOCK
    scale = 1.0 / math.sqrt(dh)
    qf = q.astype(jnp.float32)
    kf = k.astype(jnp.float32)
    vf = v.astype(jnp.float32)
    q_blocks = qf.reshape(b, h, n_blk, Q_BLOCK, dh).transpose(2, 0, 1, 3, 4)
    key_pos = jnp.arange(s)

    def one_block(args):
        qb, blk = args
        z = jnp.einsum('bhqd,bhkd->bhqk', qb, kf) * scale
        q_pos = blk * Q_BLOCK + jnp.arange(Q_BLOCK)
        causal = key_pos[None, :] < q_pos[:, None]
        log_beta = jax.nn.log_sigmoid(z)
        log_1m = jnp.where(causal, jax.nn.log_sigmoid(-z), 0.0)
        suffix = lax.cumsum(log_1m, axis=3, reverse=True) - log_1m
        weights = jnp.where(causal, jnp.exp(log_beta + suffix), 0.0)
        return jnp.einsum('bhqk,bhkd->bhqd', weights, vf)

    out = lax.map(one_block, (q_blocks, jnp.arange(n_blk)))
    out = out.transpose(1, 0, 3, 2, 4).reshape(b, s, h * dh)
    return out.astype(q.dtype)

def causal_depthwise_conv(x, w, bias):
    s = x.shape[1]
    xp = jnp.pad(x, ((0, 0), (CONV_WIDTH - 1, 0), (0, 0)))
    out = sum(xp[:, k:k + s, :] * w[k] for k in range(CONV_WIDTH))
    return out + bias

def block_diag_linear(x, w, bias):
    b, s, c = x.shape
    xr = x.reshape(b, s, N_LRU_BLOCKS, LRU_BLOCK)
    return jnp.einsum('bsnc,ncd->bsnd', xr, w).reshape(b, s, c) + bias

def rg_lru(x, w_rgate, b_rgate, w_igate, b_igate, lru_lambda):
    xf = x.astype(jnp.float32)
    r = jax.nn.sigmoid(block_diag_linear(x, w_rgate, b_rgate).astype(jnp.float32))
    i = jax.nn.sigmoid(block_diag_linear(x, w_igate, b_igate).astype(jnp.float32))
    log_a = LRU_C * r * jax.nn.log_sigmoid(lru_lambda.astype(jnp.float32))
    a = jnp.exp(log_a)
    mult = jnp.sqrt(-jnp.expm1(2.0 * log_a))
    bterm = mult * (i * xf)

    def combine(left, right):
        a_l, b_l = left
        a_r, b_r = right
        return a_l * a_r, a_r * b_l + b_r

    _, h = lax.associative_scan(combine, (a, bterm), axis=1)
    return h.astype(x.dtype)

def hybrid_mixer(hn, w_in, conv_w, conv_b, w_rgate, b_rgate, w_igate, b_igate, lru_lambda,
                 attn_out_norm, lru_out_norm, w_out):
    b, s, _ = hn.shape
    proj = hn @ w_in
    q, k, v, x_lru, g_lru = jnp.split(
        proj, [ATTN_WIDTH, 2 * ATTN_WIDTH, 3 * ATTN_WIDTH, 3 * ATTN_WIDTH + LRU_WIDTH], axis=-1)

    def heads(t):
        return t.reshape(b, s, N_ATTN_HEADS, HEAD_DIM).transpose(0, 2, 1, 3)

    y_attn = stick_breaking_attention(heads(q), heads(k), heads(v))

    xc = causal_depthwise_conv(x_lru, conv_w, conv_b)
    h = rg_lru(xc, w_rgate, b_rgate, w_igate, b_igate, lru_lambda)
    y_lru = h * jax.nn.gelu(g_lru)

    y = jnp.concatenate([rmsnorm(y_attn, attn_out_norm), rmsnorm(y_lru, lru_out_norm)], axis=-1)
    return y @ w_out

def swiglu_ffn(hn, w_gate, w_up, w_down):
    return (jax.nn.silu(hn @ w_gate) * (hn @ w_up)) @ w_down

def setup_inputs(seed: int = 0) -> dict:
    key = jax.random.key(seed)
    ks = jax.random.split(key, 20)
    f32 = jnp.float32

    def normal(k, shape, fan_in):
        return jax.random.normal(k, shape, f32) * (fan_in ** -0.5)

    def gain(k, shape):
        return 1.0 + 0.02 * jax.random.normal(k, shape, f32)

    def small(k, shape):
        return 0.01 * jax.random.normal(k, shape, f32)

    x = jax.random.normal(ks[0], (BATCH, SEQ, D_MODEL), f32)
    u = jax.random.uniform(ks[10], (DEPTH, LRU_WIDTH), f32, 0.9, 0.999)
    a0 = u ** (1.0 / LRU_C)
    lru_lambda = jnp.log(a0) - jnp.log1p(-a0)
    return {
        "x": x,
        "pre_mix_norm": gain(ks[1], (DEPTH, D_MODEL)),
        "post_mix_norm": gain(ks[2], (DEPTH, D_MODEL)),
        "pre_ffn_norm": gain(ks[3], (DEPTH, D_MODEL)),
        "post_ffn_norm": gain(ks[4], (DEPTH, D_MODEL)),
        "w_in": normal(ks[5], (DEPTH, D_MODEL, IN_WIDTH), D_MODEL),
        "conv_w": normal(ks[6], (DEPTH, CONV_WIDTH, LRU_WIDTH), CONV_WIDTH),
        "conv_b": small(ks[7], (DEPTH, LRU_WIDTH)),
        "w_rgate": normal(ks[8], (DEPTH, N_LRU_BLOCKS, LRU_BLOCK, LRU_BLOCK), LRU_BLOCK),
        "b_rgate": small(ks[9], (DEPTH, LRU_WIDTH)),
        "w_igate": normal(ks[11], (DEPTH, N_LRU_BLOCKS, LRU_BLOCK, LRU_BLOCK), LRU_BLOCK),
        "b_igate": small(ks[12], (DEPTH, LRU_WIDTH)),
        "lru_lambda": lru_lambda,
        "attn_out_norm": gain(ks[13], (DEPTH, ATTN_WIDTH)),
        "lru_out_norm": gain(ks[14], (DEPTH, LRU_WIDTH)),
        "w_out": normal(ks[15], (DEPTH, MIX_WIDTH, D_MODEL), MIX_WIDTH),
        "w_ffn_gate": normal(ks[16], (DEPTH, D_MODEL, D_FF), D_MODEL),
        "w_ffn_up": normal(ks[17], (DEPTH, D_MODEL, D_FF), D_MODEL),
        "w_ffn_down": normal(ks[18], (DEPTH, D_FF, D_MODEL), D_FF),
    }

def reference(x, pre_mix_norm, post_mix_norm, pre_ffn_norm, post_ffn_norm, w_in, conv_w, conv_b,
              w_rgate, b_rgate, w_igate, b_igate, lru_lambda, attn_out_norm, lru_out_norm, w_out,
              w_ffn_gate, w_ffn_up, w_ffn_down):
    for l in range(DEPTH):
        hn = rmsnorm(x, pre_mix_norm[l])
        m = hybrid_mixer(hn, w_in[l], conv_w[l], conv_b[l], w_rgate[l], b_rgate[l], w_igate[l],
                         b_igate[l], lru_lambda[l], attn_out_norm[l], lru_out_norm[l], w_out[l])
        x = x + rmsnorm(m, post_mix_norm[l])
        hn = rmsnorm(x, pre_ffn_norm[l])
        f = swiglu_ffn(hn, w_ffn_gate[l], w_ffn_up[l], w_ffn_down[l])
        x = x + rmsnorm(f, post_ffn_norm[l])
    return x


_drawn_inputs = setup_inputs


def setup_inputs(seed=0):
    import zlib

    import numpy as np

    out = dict(_drawn_inputs(seed))
    spreads = {}
    factors = {'post_mix_norm': 3.351,
     'pre_ffn_norm': 3.552,
     'post_ffn_norm': 17.421,
     'b_rgate': 26.828,
     'b_igate': 8.0,
     'attn_out_norm': 15.42,
     'lru_out_norm': 16.86}
    for name, (base, spread) in spreads.items():
        noise = np.random.default_rng([zlib.crc32(name.encode()), seed]).standard_normal(out[name].shape)
        drawn = base * np.exp(spread * noise) if base else spread * noise
        out[name] = __import__('jax').numpy.asarray(drawn.astype(out[name].dtype))
    for name, factor in factors.items():
        out[name] = (out[name] * factor).astype(out[name].dtype)
    return out
```

```python
from contextlib import ExitStack

import concourse.bass as bass
from concourse import mybir

F32 = mybir.dt.float32
F32R = mybir.dt.float32r
ALU = mybir.AluOpType
ACT = mybir.ActivationFunctionType
AX_X = mybir.AxisListType.X

P = 128
HEADS = 8
PARAMS = 8
EPS = 1e-6
LRU_C = 8.0
CONV = 4
NEVER = -1.0e30


class Steps:

    def __init__(self, engine, semaphore):
        self.engine, self.semaphore = engine, semaphore
        self.before, self.here = 0, 0

    def __call__(self, instruction):
        self.here += 1
        instruction.then_inc(self.semaphore, 1)
        self.engine.wait_ge(self.semaphore, self.before + self.here)

    def loop(self, index, first, per_pass):
        self.start = self.before + self.here
        self.before, self.here = index * per_pass + (self.start - first * per_pass), 0

    def end(self, passes, per_pass):
        assert self.here == per_pass, (self.here, per_pass)
        self.before, self.here = self.start + passes * per_pass, 0


def decoder_layer(nc, x, g_pre_mix, g_post_mix, g_pre_ffn, g_post_ffn, w_in, lru_params, w_rgate,
                  w_igate, y_gains, w_out, w_gate, w_up, w_down, out):
    SEQ, D = x.shape
    TB = SEQ // P
    KT = D // P
    W = D // HEADS // 2
    HALF = D // 2
    NC = 512
    NN = D // NC
    KC = NC // P
    CH = KC * NC
    GROUPS = w_gate.shape[1] // NC
    SCALE = float(W) ** -0.5
    assert W == P and CH == KT * P and SEQ == 512 and KT == 16
    C_OUT = 5 * HEADS
    C_FFN = C_OUT + NN * (KT // KC)
    C_LAST = C_FFN + 12 * GROUPS
    OFF = {0: (512, 384), 2: (896, 128), 1: (1024, 256)}
    SC = 1280

    ctx = ExitStack()
    with ctx:
        def sb(name, shape, dt=F32, stack=ctx):
            return stack.enter_context(nc.sbuf_tensor(name, shape, dt))

        def sem(name):
            return ctx.enter_context(nc.semaphore(name))

        bank = [ctx.enter_context(nc.psum_tensor(f"bank{i}", [P, 512], F32)) for i in range(3)]
        scores3 = ctx.enter_context(nc.psum_tensor("scores3", [P, 3, 512], F32))
        bank += [scores3[:, i, :] for i in range(3)]
        bank += [ctx.enter_context(nc.psum_tensor(f"bank{i}", [P, 512], F32)) for i in (6, 7)]
        bank = [b[:, :] for b in bank]
        z_all = scores3[:, :, :].rearrange("p a b -> p (a b)")
        SET_A = [bank[i] for i in (0, 1, 2, 7)]
        SET_B = [bank[i] for i in (3, 4, 5, 6)]

        w_raw = sb("w_raw", [P, 2, CH])
        w_hi = sb("w_hi", [P, 2, CH], F32R)
        w_lo = sb("w_lo", [P, 2, CH], F32R)
        act_hi = sb("act_hi", [P, KT, SEQ], F32R)
        act_lo = sb("act_lo", [P, KT, SEQ], F32R)
        ident = sb("ident", [P, P])
        ones = sb("ones", [P, 1])
        ygain = sb("ygain", [P, KT])
        stat = sb("stat", [P, 64])

        with ExitStack() as head:
            x_in = sb("x_in", [P, 2, D], stack=head)
            x_norm = sb("x_norm", [P, 2, D], stack=head)
            gain0 = sb("gain0", [P, D], stack=head)
            square0 = sb("square0", [P, D], stack=head)
        with ExitStack() as mix:
            y_raw = sb("y_raw", [P, KT, SEQ], stack=mix)
            ssq = sb("ssq", [P, 2, SEQ], stack=mix)
            prm_all = sb("prm_all", [P, HEADS, PARAMS + 2], stack=mix)
            prm = sb("prm", [P, 2, PARAMS + 2], stack=mix)
            gate_w = sb("gate_w", [P, 2, 2, P], stack=mix)
            tri_neg = sb("tri_neg", [P, P], stack=mix)
            ones_neg = sb("ones_neg", [P, P], stack=mix)
            later = sb("later", [P, 4, P], stack=mix)
            never = sb("never", [P, 4, P], stack=mix)
            qT = sb("qT", [P, SEQ], stack=mix)
            kT = sb("kT", [P, SEQ], stack=mix)
            vT = sb("vT", [P, SEQ], stack=mix)
            v_nat = sb("v_nat", [P, TB, P], stack=mix)
            soft = sb("soft", [P, SC], stack=mix)
            stick = sb("stick", [P, SC], stack=mix)
            weight = sb("weight", [P, SC], stack=mix)
            xs = sb("xs", [P, CONV - 1 + SEQ], stack=mix)
            xc = sb("xc", [P, SEQ], stack=mix)
            r_t = sb("r_t", [P, SEQ], stack=mix)
            i_t = sb("i_t", [P, SEQ], stack=mix)
            u_t = sb("u_t", [P, SEQ], stack=mix)
            a_t = sb("a_t", [P, SEQ], stack=mix)
            d_t = sb("d_t", [P, SEQ], stack=mix)
            gelu_t = sb("gelu_t", [P, SEQ], stack=mix)
            ya_t = sb("ya_t", [P, SEQ], stack=mix)
            yl_t = sb("yl_t", [P, SEQ], stack=mix)
            sq_t = sb("sq_t", [P, SEQ], stack=mix)
        with ExitStack() as tail:
            mixed = sb("mixed", [P, TB, D], stack=tail)
            resid = sb("resid", [P, TB, D], stack=tail)
            square = sb("square", [P, NC], stack=tail)
            with ExitStack() as mid:
                gain1 = sb("gain1", [P, D], stack=mid)
                gain2 = sb("gain2", [P, D], stack=mid)
            with ExitStack() as ffn:
                h_hi = sb("h_hi", [P, KC, SEQ], F32R, stack=ffn)
                h_lo = sb("h_lo", [P, KC, SEQ], F32R, stack=ffn)
                h_raw = sb("h_raw", [P, KC, SEQ], stack=ffn)
            with ExitStack() as end:
                sb("over_h_hi", [P, KC, SEQ], F32R, stack=end)
                sb("over_h_lo", [P, KC, SEQ], F32R, stack=end)
                gain3 = sb("gain3", [P, D], stack=end)

        raw_loaded = [sem("raw_loaded0"), sem("raw_loaded1")]
        hi_ready = sem("hi_ready")
        split_ready = sem("split_ready")
        chunk_used = sem("chunk_used")
        x_loaded = [sem("x_loaded0"), sem("x_loaded1")]
        gain0_loaded = sem("gain0_loaded")
        small_loaded = sem("small_loaded")
        consts_ready = sem("consts_ready")
        zeros_ready = sem("zeros_ready")
        coef_ready = sem("coef_ready")
        squared = sem("squared")
        mean_ready = sem("mean_ready")
        root_ready = sem("root_ready")
        normed = sem("normed")
        turned = sem("turned")
        turned_hi = sem("turned_hi")
        turned_lo = sem("turned_lo")
        q_out, k_out, v_out = sem("q_out"), sem("k_out"), sem("v_out")
        scores_ready = sem("scores_ready")
        soft_ready = sem("soft_ready")
        stick_ready = sem("stick_ready")
        v_turned = sem("v_turned")
        v_ready = sem("v_ready")
        logw_ready = sem("logw_ready")
        logd_ready = sem("logd_ready")
        weight_ready = sem("weight_ready")
        av_ready = sem("av_ready")
        ya_ready = sem("ya_ready")
        ya_stored = sem("ya_stored")
        params_ready = sem("params_ready")
        gate_w_loaded = [sem("gate_w_loaded0"), sem("gate_w_loaded1")]
        x_out, g_out = sem("x_out"), sem("g_out")
        xc_ready = sem("xc_ready")
        gates_ready = sem("gates_ready")
        ri_ready = sem("ri_ready")
        ua_ready = sem("ua_ready")
        v2_ready = sem("v2_ready")
        mult_ready = sem("mult_ready")
        yl_ready = sem("yl_ready")
        yl_stored = sem("yl_stored")
        y_hi = sem("y_hi")
        y_lo = sem("y_lo")
        ssq_ready = sem("ssq_ready")
        rstd_ready = sem("rstd_ready")
        last_out = sem("last_out")
        mix_a = sem("mix_a")
        mix_b = sem("mix_b")
        resid_loaded = sem("resid_loaded")
        gains_loaded = sem("gains_loaded")
        scaled = sem("scaled")
        resid_ready = sem("resid_ready")
        silu_ready = sem("silu_ready")
        h_ready = sem("h_ready")
        h_hi_ready = sem("h_hi_ready")
        h_lo_ready = sem("h_lo_ready")
        down_out = sem("down_out")
        final_ready = sem("final_ready")
        stored = sem("stored")
        act_steps, dve_steps, pool_steps = sem("act_steps"), sem("dve_steps"), sem("pool_steps")

        block = ctx.enter_context(nc.Block())

        def rows(w, r0, c0):
            return w[bass.ds(r0, NC), bass.ds(c0, NC)].rearrange("(k p) n -> p k n", p=P)

        def lead(h):
            return w_in[:, bass.ds(h, P)].rearrange("(k p) n -> p k n", p=P)

        @block.sync
        def _(sp):
            def load(half, off, src, k):
                if not (isinstance(half, int) and 2 * half + off < 2):
                    sp.wait_ge(split_ready, 2 * half + off - 1)
                dst = w_raw[:, off % 2, :].rearrange("p (k n) -> p k n", k=k)
                sp.dma_start(dst, src).then_inc(raw_loaded[off % 2], 16)

            def load_x(tb):
                if tb >= 2:
                    sp.wait_ge(normed, tb - 1)
                sp.dma_start(x_in[:, tb % 2, :], x[tb * P:(tb + 1) * P, :]).then_inc(x_loaded[tb % 2], 16)

            def load_gates(h, slot):
                for n, w in enumerate((w_rgate, w_igate)):
                    sp.dma_start(gate_w[:, slot, n, :], w[bass.ds(h, 1)].rearrange("a c d -> (a c) d"))\
                        .then_inc(gate_w_loaded[slot], 16)

            load_x(0)
            load_x(1)
            sp.dma_start(gain0[:, :], g_pre_mix.partition_broadcast(P)).then_inc(gain0_loaded, 16)
            load(0, 0, lead(0), KT)
            load(0, 1, lead(HALF), KT)
            load_x(2)
            load_x(3)
            sp.wait_ge(turned, KC * TB)
            sp.dma_start(prm_all[:, :, 0:PARAMS], lru_params).then_inc(small_loaded, 16)
            sp.dma_start(ygain[:, :], y_gains).then_inc(small_loaded, 16)
            load_gates(0, 0)
            load_gates(1, 1)

            def head_pair(half, h0, last):
                for u in range(2):
                    for j in range(5):
                        off = 5 * u + 2 + j
                        if j < 3:
                            load(half, off, lead((h0 + u) * P + (j + 2) * HALF), KT)
                        elif not (last and u == 1):
                            load(half, off, lead((h0 + u + 1) * P + (j - 3) * HALF), KT)
                        else:
                            load(half, off, rows(w_out, (j - 3) * NC, 0), KC)
                    if not last:
                        sp.wait_ge(gates_ready, h0 + u + 1)
                        load_gates(h0 + u + 2, u)

            with sp.Fori(0, HEADS // 2 - 1) as t:
                head_pair(5 * t, 2 * t, False)
            head_pair(5 * (HEADS // 2 - 1), HEADS - 2, True)
            for c in range(C_OUT + 2, C_FFN):
                n, kc = divmod(c - C_OUT, KC)
                load(c // 2, c % 2, rows(w_out, kc * NC, n * NC), KC)
                if c == C_OUT + 6:
                    sp.wait_ge(rstd_ready, 2)
                    sp.dma_start(gain1[:, :], g_post_mix.partition_broadcast(P)).then_inc(gains_loaded, 16)
                    sp.dma_start(gain2[:, :], g_pre_ffn.partition_broadcast(P)).then_inc(gains_loaded, 16)
                    sp.dma_start(resid[:, :, :], x.rearrange("(t p) d -> p t d", p=P)).then_inc(resid_loaded, 16)

            def load_in(half, off, w, i):
                for kc in range(KC):
                    load(half, off + kc, rows(w, kc * NC, i * NC), KC)

            def load_down(half, off, i):
                for n in range(NN):
                    load(half, off + n, rows(w_down, i * NC, n * NC), KC)

            load_in(C_FFN // 2, 0, w_gate, 0)
            load_in(C_FFN // 2, 4, w_up, 0)
            with sp.Fori(1, GROUPS) as i:
                half = C_FFN // 2 - 2 + 6 * i
                load_in(half, 0, w_gate, i)
                load_down(half, 4, i - 1)
                load_in(half, 8, w_up, i)
            load_down((C_LAST - 4) // 2, 0, GROUPS - 1)
            sp.wait_ge(h_lo_ready, KC * GROUPS)
            sp.dma_start(gain3[:, :], g_post_ffn.partition_broadcast(P)).then_inc(gains_loaded, 16)
            for tb in range(TB):
                sp.wait_ge(final_ready, tb + 1)
                sp.dma_start(out[tb * P:(tb + 1) * P, :], mixed[:, tb, :]).then_inc(stored, 16)
            sp.wait_ge(stored, 16 * TB)

        @block.tensor
        def _(pe):
            def products(ps, lhs, rhs, start, stop):
                (lh, ll), (rh, rl) = lhs, rhs
                pe.matmul(ps, lh, rh, start=start, stop=False)
                pe.matmul(ps, lh, rl, start=False, stop=False)
                return pe.matmul(ps, ll, rh, start=False, stop=stop)

            def column_tile(half, off, ps):
                pe.wait_ge(split_ready, 2 * half + off + 1)
                for kt in range(KT):
                    cols = slice(kt * P, (kt + 1) * P)
                    mm = products(ps, (w_hi[:, off % 2, cols], w_lo[:, off % 2, cols]),
                                  (act_hi[:, kt, :], act_lo[:, kt, :]), kt == 0, kt == KT - 1)
                mm.then_inc(chunk_used, 1)

            def turn(source, banks, n0, since):
                for q in range(KC):
                    n = n0 + q
                    if n >= since + len(banks):
                        pe.wait_ge(turned_lo, n - len(banks) + 1)
                    for f in range(4):
                        kt = 4 * q + f
                        mm = pe.transpose(banks[n % len(banks)][:, f * P:(f + 1) * P],
                                          source[:, kt * P:(kt + 1) * P], ident[:, :])
                    mm.then_inc(turned, 1)

            pe.wait_ge(consts_ready, 1)
            for tb in range(TB):
                pe.wait_ge(normed, tb + 1)
                turn(x_norm[:, tb % 2, :], bank, KC * tb, 0)
            pe.wait_ge(turned_lo, KC * TB)

            def diag(t, b):
                return t[:, b * P:(b + 1) * P]

            def scores(h):
                pe.wait_ge(q_out, h + 1)
                pe.wait_ge(k_out, h + 1)
                for b in range(TB):
                    pe.matmul(diag(z_all, b), diag(kT, b), diag(qT, b), start=(b == 0), stop=False,
                              skip_group_check=True)
                for b, (o, n) in OFF.items():
                    mm = pe.matmul(z_all[:, o:o + n], diag(kT, b), qT[:, SEQ - n:SEQ],
                                   start=b < 2, stop=False, skip_group_check=True)
                mm.then_inc(scores_ready, 1)

            def turn_v(h):
                pe.wait_ge(v_out, h + 1)
                if not (isinstance(h, int) and h == 0):
                    pe.wait_ge(ya_ready, h)
                for b in range(TB):
                    mm = pe.transpose(diag(bank[6], b), diag(vT, b), ident[:, :])
                mm.then_inc(v_turned, 1)

            def suffix(h):
                pe.wait_ge(stick_ready, h + 1)
                for kb in range(TB):
                    for jb in range(kb, TB):
                        lhs = (tri_neg if jb == kb else ones_neg)[:, :]
                        if jb == kb:
                            outs = [(diag(z_all, kb), diag(stick, kb))]
                            if kb < TB - 1:
                                o, n = OFF[kb]
                                outs.append((z_all[:, o:o + n], stick[:, o:o + n]))
                        else:
                            o, n = OFF[kb]
                            at = o + (jb - kb - 1) * P
                            outs = [(z_all[:, at:at + P], diag(stick, jb))]
                            if jb < TB - 1:
                                oj, nj = OFF[jb]
                                outs.append((z_all[:, at + P:o + n], stick[:, oj:oj + nj]))
                        for ps, rhs in outs:
                            mm = pe.matmul(ps, lhs, rhs, start=False, stop=(kb == jb == TB - 1),
                                           skip_group_check=True)
                mm.then_inc(logw_ready, 1)

            def attend(h):
                pe.wait_ge(v_ready, h + 1)
                pe.wait_ge(weight_ready, 2 * (h + 1))
                for b in range(TB):
                    mm = pe.matmul(diag(bank[6], b), v_nat[:, b, :], diag(weight, b), start=(b == 0),
                                   stop=(b == TB - 1), skip_group_check=True)
                    if b < TB - 1:
                        o, n = OFF[b]
                        pe.matmul(bank[6][:, SEQ - n:SEQ], v_nat[:, b, :], weight[:, o:o + n],
                                  start=False, stop=False, skip_group_check=True)
                mm.then_inc(av_ready, 1)

            def gates(h, turn_no, slot):
                pe.wait_ge(xc_ready, h + 1)
                pe.wait_ge(gate_w_loaded[slot], 32 * turn_no)
                for n in range(2):
                    mm = pe.matmul(bank[3 + n], gate_w[:, slot, n, :], xc[:, :], start=True, stop=True)
                mm.then_inc(gates_ready, 1)

            def head_of(half, h0, t, u, last):
                h, off = h0 + u, 5 * u
                first = isinstance(h, int) and h == 0
                if not first:
                    pe.wait_ge(x_out, h)
                column_tile(half, off + 1, bank[1])
                pe.wait_ge(q_out, h + 1)
                column_tile(half, off + 2, bank[0])
                if not first:
                    pe.wait_ge(ri_ready, 2 * h)
                scores(h)
                column_tile(half, off + 3, bank[1])
                turn_v(h)
                if not first:
                    pe.wait_ge(g_out, h)
                column_tile(half, off + 4, bank[2])
                suffix(h)
                if not last:
                    column_tile(half, off + 5, bank[0])
                    attend(h)
                    gates(h, t + 1, u)

            column_tile(0, 0, bank[0])
            pe.wait_ge(consts_ready, 2)
            head_of(0, 0, 0, 0, False)
            head_of(0, 0, 0, 1, False)
            with pe.Fori(1, HEADS // 2 - 1) as t:
                head_of(5 * t, 2 * t, t, 0, False)
                head_of(5 * t, 2 * t, t, 1, False)
            t = HEADS // 2 - 1
            head_of(5 * t, 2 * t, t, 0, False)
            head_of(5 * t, 2 * t, t, 1, True)

            def row_blocks(c, lhs, k0, banks, start, stop, free=None, inputs=None, sem_each=None):
                half, off = c
                pe.wait_ge(split_ready, 2 * half + off + 1)
                for tb in range(TB):
                    if free is not None:
                        free(tb)
                    for k in range(KC):
                        if inputs is not None and tb == 0:
                            inputs(k)
                        toks = slice(tb * P, (tb + 1) * P)
                        cols = slice(k * NC, (k + 1) * NC)
                        mm = products(banks[tb], (lhs[0][:, k0 + k, toks], lhs[1][:, k0 + k, toks]),
                                      (w_hi[:, off % 2, cols], w_lo[:, off % 2, cols]),
                                      start and k == 0, stop and k == KC - 1)
                    if sem_each is not None:
                        mm.then_inc(sem_each, 1)
                if sem_each is None:
                    mm.then_inc(chunk_used, 1)

            act = (act_hi, act_lo)
            for n in range(NN):
                for kc in range(KC):
                    c = C_OUT + KC * n + kc
                    banks, read = (SET_A, mix_a) if kc < 2 else (SET_B, mix_b)

                    def free(tb, n=n, kc=kc, read=read):
                        if n >= 1 and kc % 2 == 0:
                            pe.wait_ge(read, TB * (n - 1) + tb + 1)
                        elif n == 0 and kc == 0:
                            pe.wait_ge(g_out, HEADS)
                        elif n == 0 and kc == 2:
                            pe.wait_ge(ri_ready, 2 * HEADS)
                            pe.wait_ge(ya_ready, HEADS)
                            pe.wait_ge(rstd_ready, 1)

                    def inputs(k, n=n, kc=kc):
                        if n == 0:
                            pe.wait_ge(y_lo, KC * kc + k + 1)

                    is_last = c == C_FFN - 1
                    row_blocks((c // 2, c % 2), act, KC * kc, banks, kc % 2 == 0, kc % 2 == 1, free,
                               inputs, last_out if is_last else None)
                    if c == C_OUT:
                        attend(HEADS - 1)
                        gates(HEADS - 1, HEADS // 2, 1)
                    if c in (C_OUT + 1, C_OUT + 2):
                        which = c - C_OUT - 1
                        pe.wait_ge((ya_stored, yl_stored)[which], HEADS)
                        if which:
                            pe.wait_ge(mix_a, TB)
                        else:
                            pe.wait_ge(ri_ready, 2 * HEADS)
                        for tb in range(TB):
                            mm = pe.matmul(bank[0 if which else 3][:, tb:tb + 1],
                                           ssq[:, which, tb * P:(tb + 1) * P], ones[:, :],
                                           start=(tb == 0), stop=(tb == TB - 1), skip_group_check=True)
                        mm.then_inc(ssq_ready, 1)
                    if c == C_OUT + 3:
                        pe.wait_ge(rstd_ready, 2)

            for tb in range(TB):
                pe.wait_ge(normed, TB + tb + 1)
                turn(mixed[:, tb, :], SET_A, KC * (TB + tb), KC * TB)
            pe.wait_ge(turned_lo, 2 * KC * TB)

            def into_ffn(half, off, banks, free):
                free()
                for kc in range(KC):
                    pe.wait_ge(split_ready, 2 * half + off + kc + 1)
                    slot = (off + kc) % 2
                    for f in range(KC):
                        for k in range(KC):
                            at = k * NC + f * P
                            mm = products(banks[f], (w_hi[:, slot, at:at + P], w_lo[:, slot, at:at + P]),
                                          (act_hi[:, KC * kc + k, :], act_lo[:, KC * kc + k, :]),
                                          kc == k == 0, kc == k + 0 == KC - 1)
                    mm.then_inc(chunk_used, 1)

            def down(half, off, i, sets, free, is_last=False):
                pe.wait_ge(h_lo_ready, KC * (i + 1))
                for n in range(NN):
                    free(n)
                    row_blocks((half, off + n), (h_hi, h_lo), 0, sets[n], True, True,
                               sem_each=last_out if is_last and n == NN - 1 else None)

            h = C_FFN // 2
            into_ffn(h, 0, SET_A, lambda: None)
            into_ffn(h, 4, SET_B, lambda: pe.wait_ge(mix_b, TB * NN))
            BABA = [SET_B, SET_A, SET_B, SET_A]

            def group(half, i, first):
                into_ffn(half, 0, SET_A, lambda: pe.wait_ge(silu_ready, KC) if first
                         else pe.wait_ge(down_out, TB * NN * (i - 1)))

                def free(n):
                    if n == 1:
                        pe.wait_ge(silu_ready, KC * (i + 1))
                    if n >= 2:
                        pe.wait_ge(down_out, TB * NN * (i - 1) + TB * (n - 1))
                down(half, 4, i - 1, BABA, free)
                into_ffn(half, 8, SET_B, lambda: pe.wait_ge(down_out, TB * NN * (i - 1) + TB * 3))

            group(h + 4, 1, True)
            with pe.Fori(2, GROUPS) as i:
                group(C_FFN // 2 - 2 + 6 * i, i, False)

            def free(n):
                if n == 0:
                    pe.wait_ge(down_out, TB * NN * (GROUPS - 1))
                if n >= 2:
                    pe.wait_ge(down_out, TB * NN * (GROUPS - 1) + TB * (n - 1))
            down((C_LAST - 4) // 2, 0, GROUPS - 1, [SET_A, SET_B, SET_A, SET_B], free, True)

        @block.scalar
        def _(act):
            step = Steps(act, act_steps)
            shift = [0]

            def used_by_pe(half, off):
                if isinstance(half, int):
                    c = 2 * half + off
                    if c == C_FFN - 1:
                        act.wait_ge(last_out, TB)
                    else:
                        act.wait_ge(chunk_used, c + 1 - (c >= C_FFN))
                else:
                    act.wait_ge(chunk_used, 2 * half + off + 1 - shift[0])

            def high(half, off):
                act.wait_ge(raw_loaded[off % 2], 16 * (half + off // 2 + 1))
                if not (isinstance(half, int) and 2 * half + off < 2):
                    used_by_pe(half, off - 2)
                nc.scalar.activation(w_hi[:, off % 2, :], w_raw[:, off % 2, :], ACT.Copy).then_inc(hi_ready, 1)

            def turned_high(n, tb, q, bnk):
                act.wait_ge(turned, n + 1)
                nc.scalar.activation(act_hi[:, 4 * q:4 * q + 4, tb * P:(tb + 1) * P],
                                     bnk.rearrange("p (f t) -> p f t", f=4), ACT.Copy).then_inc(turned_hi, 1)

            high(0, 0)
            for tb in range(TB):
                act.wait_ge(x_loaded[tb % 2], 16 * (tb // 2 + 1))
                if tb:
                    act.wait_ge(squared, tb)
                nc.scalar.activation(square0[:, :], x_in[:, tb % 2, :], ACT.Square,
                                     accum_out=stat[:, tb:tb + 1]).then_inc(squared, 1)
                act.wait_ge(mean_ready, tb + 1)
                nc.scalar.activation(stat[:, 8 + tb:9 + tb], stat[:, 4 + tb:5 + tb], ACT.Sqrt)\
                    .then_inc(root_ready, 1)
                for q in range(KC):
                    turned_high(KC * tb + q, tb, q, bank[(KC * tb + q) % 8])
            lam = prm_all[:, :, PARAMS - 1]
            pos, neg = prm_all[:, :, PARAMS], prm_all[:, :, PARAMS + 1]
            act.wait_ge(small_loaded, 32)
            step(nc.scalar.activation(pos, lam, ACT.Abs))
            step(nc.scalar.activation(pos, pos, ACT.Exp, scale=-1.0))
            step(nc.scalar.activation(pos, pos, ACT.Ln, bias=1.0))
            nc.scalar.activation(neg, lam, ACT.Relu, scale=-1.0).then_inc(coef_ready, 1)
            high(0, 1)

            def out_of(half, off, dst, bnk, done, scale=1.0):
                used_by_pe(half, off)
                nc.scalar.activation(dst, bnk, ACT.Copy, scale=scale).then_inc(done, 1)

            def q_in(half, off, h):
                if not (isinstance(h, int) and h == 0):
                    act.wait_ge(scores_ready, h)
                out_of(half, off, qT[:, :], bank[0], q_out, SCALE)

            def y_high(ft):
                nc.scalar.activation(act_hi[:, ft, :], y_raw[:, ft, :], ACT.Copy,
                                     scale=ygain[:, ft:ft + 1]).then_inc(y_hi, 1)

            PER_HEAD = 2

            def head_of(half, h0, u, last=False):
                h, off = h0 + u, 5 * u
                first = isinstance(h, int) and h == 0
                if not first:
                    act.wait_ge(scores_ready, h)
                out_of(half, off + 1, kT[:, :], bank[1], k_out)
                high(half, off + 3)
                if not first:
                    act.wait_ge(v_turned, h)
                out_of(half, off + 2, vT[:, :], bank[0], v_out)
                high(half, off + 4)
                act.wait_ge(scores_ready, h + 1)
                if not first:
                    act.wait_ge(stick_ready, h)
                step(nc.scalar.activation(soft[:, :], z_all[:, 0:SC], ACT.Abs))
                step(nc.scalar.activation(soft[:, :], soft[:, :], ACT.Exp, scale=-1.0))
                nc.scalar.activation(soft[:, :], soft[:, :], ACT.Ln, bias=1.0).then_inc(soft_ready, 1)
                if not first:
                    act.wait_ge(xc_ready, h)
                out_of(half, off + 3, xs[:, CONV - 1:CONV - 1 + SEQ], bank[1], x_out)
                high(half, off + 5)
                if last:
                    used_by_pe(half, off + 4)
                    for ft in range(KC):
                        y_high(ft)
                act.wait_ge(logw_ready, h + 1)
                if not first:
                    act.wait_ge(av_ready, h)
                nc.scalar.activation(weight[:, 512:SC], z_all[:, 512:SC], ACT.Exp).then_inc(weight_ready, 1)
                act.wait_ge(logd_ready, h + 1)
                nc.scalar.activation(weight[:, 0:512], weight[:, 0:512], ACT.Exp).then_inc(weight_ready, 1)
                if not first:
                    act.wait_ge(yl_ready, h)
                used_by_pe(half, off + 4)
                nc.scalar.activation(gelu_t[:, :], bank[2], ACT.Gelu_apprx_tanh).then_inc(g_out, 1)
                high(half, off + 6)
                if not last:
                    q_in(half, off + 5, h + 1)
                else:
                    for ft in range(KC, 2 * KC):
                        act.wait_ge(ya_stored, ft + 1)
                        y_high(ft)
                high(half, off + 7)
                act.wait_ge(gates_ready, h + 1)
                act.wait_ge(params_ready, h + 1)
                pr = prm[:, u, :]
                nc.scalar.activation(r_t[:, :], bank[3], ACT.Sigmoid, bias=pr[:, 5:6]).then_inc(ri_ready, 1)
                nc.scalar.activation(i_t[:, :], bank[4], ACT.Sigmoid, bias=pr[:, 6:7]).then_inc(ri_ready, 1)
                act.wait_ge(ri_ready, 2 * h + 2)
                nc.scalar.activation(u_t[:, :], r_t[:, :], ACT.Tanh, scale=pr[:, 8:9]).then_inc(ua_ready, 1)
                nc.scalar.activation(a_t[:, :], r_t[:, :], ACT.Exp, scale=pr[:, 9:10]).then_inc(ua_ready, 1)
                act.wait_ge(v2_ready, h + 1)
                nc.scalar.activation(d_t[:, :], d_t[:, :], ACT.Sqrt).then_inc(mult_ready, 1)

            q_in(0, 0, 0)
            high(0, 2)
            head_of(0, 0, 0)
            head_of(0, 0, 1)
            with act.Fori(1, HEADS // 2 - 1) as t:
                step.loop(t, 1, 2 * PER_HEAD)
                head_of(5 * t, 2 * t, 0)
                head_of(5 * t, 2 * t, 1)
            step.end(HEADS // 2 - 2, 2 * PER_HEAD)
            t = HEADS // 2 - 1
            head_of(5 * t, 2 * t, 0)
            head_of(5 * t, 2 * t, 1, True)

            def rstd(which):
                act.wait_ge(mean_ready, TB + which + 1)
                nc.scalar.activation(stat[:, 16 + 4 * which:20 + 4 * which],
                                     stat[:, 24 + 4 * which:28 + 4 * which], ACT.Sqrt).then_inc(root_ready, 1)

            for n in range(NN):
                for kc in range(KC):
                    c = C_OUT + KC * n + kc
                    if c + 1 >= C_OUT + 3:
                        high((c + 1) // 2, (c + 1) % 2)
                    if n == 0 and kc == 1:
                        rstd(0)
                        for ft in range(2 * KC, 4 * KC):
                            act.wait_ge(yl_stored, ft - 2 * KC + 1)
                            y_high(ft)
                    if kc == 2:
                        used_by_pe((c - 1) // 2, (c - 1) % 2)
                        for tb in range(TB):
                            if n == 0 and tb == 0:
                                act.wait_ge(rstd_ready, 1)
                                act.wait_ge(y_lo, KT)
                            nc.scalar.activation(mixed[:, tb, n * NC:(n + 1) * NC], SET_A[tb], ACT.Copy,
                                                 scale=stat[:, 32 + tb:33 + tb]).then_inc(mix_a, 1)
                        if n == 0:
                            rstd(1)
                    if n >= 1 and kc == 1:
                        for tb in range(TB):
                            act.wait_ge(mix_b, TB * (n - 1) + tb + 1)
                            step(nc.scalar.activation(square[:, :], mixed[:, tb, (n - 1) * NC:n * NC],
                                                      ACT.Square,
                                                      accum_out=stat[:, 40 + 4 * tb + n - 1:41 + 4 * tb + n - 1]))
            for tb in range(TB):
                n = NN - 1
                act.wait_ge(mix_b, TB * n + tb + 1)
                nc.scalar.activation(square[:, :], mixed[:, tb, n * NC:D], ACT.Square,
                                     accum_out=stat[:, 40 + 4 * tb + n:41 + 4 * tb + n]).then_inc(squared, 1)
                act.wait_ge(mean_ready, TB + 2 + 2 * tb + 1)
                nc.scalar.activation(stat[:, 8 + tb:9 + tb], stat[:, 4 + tb:5 + tb], ACT.Sqrt)\
                    .then_inc(root_ready, 1)
                act.wait_ge(resid_ready, tb + 1)
                nc.scalar.activation(mixed[:, tb, :], resid[:, tb, :], ACT.Square,
                                     accum_out=stat[:, tb:tb + 1]).then_inc(squared, 1)
                act.wait_ge(mean_ready, TB + 2 + 2 * tb + 2)
                nc.scalar.activation(stat[:, 8 + tb:9 + tb], stat[:, 4 + tb:5 + tb], ACT.Sqrt)\
                    .then_inc(root_ready, 1)
                for q in range(KC):
                    if q == 0:
                        act.wait_ge(last_out, TB)
                    turned_high(KC * (TB + tb) + q, tb, q, SET_A[q])
                if tb == 0:
                    high(C_FFN // 2, 1)

            def gate_step(half, off, i, skip_first=False):
                for kc in range(KC):
                    high(half, off + kc + 1)

            def silu(half, off, i):
                used_by_pe(half, off)
                if not (isinstance(i, int) and i == 0):
                    act.wait_ge(h_lo_ready, KC * i)
                for f in range(KC):
                    nc.scalar.activation(h_raw[:, f, :], SET_A[f], ACT.Silu).then_inc(silu_ready, 1)

            def h_high(i):
                for f in range(KC):
                    act.wait_ge(h_ready, KC * i + f + 1)
                    nc.scalar.activation(h_hi[:, f, :], h_raw[:, f, :], ACT.Copy).then_inc(h_hi_ready, 1)

            F = C_FFN // 2
            for kc in range(1, KC):
                high(F, kc + 1)
            high(F, 5)
            silu(F, 3, 0)
            for kc in range(1, KC):
                high(F, 4 + kc + 1)

            def group(half, i):
                for kc in range(KC):
                    high(half, kc + 1)
                    if kc == 0:
                        h_high(i - 1)
                for n in range(NN):
                    high(half, 4 + n + 1)
                    if n == 0:
                        silu(half, 3, i)
                for kc in range(KC - 1):
                    high(half, 8 + kc + 1)

            shift[0] = 1

            def whole_group(half, i, last):
                group(half, i)
                if not last:
                    high(half, 12)

            with act.Fori(1, GROUPS - 1) as i:
                whole_group(F - 2 + 6 * i, i, False)
            half = F - 2 + 6 * (GROUPS - 1)
            whole_group(half, GROUPS - 1, False)
            high(half, 13)
            h_high(GROUPS - 1)
            high(half, 14)
            high(half, 15)
            for n in range(NN):
                for tb in range(TB):
                    act.wait_ge(down_out, TB * NN * (GROUPS - 1) + TB * n + tb + 1)
                    at = 40 + 4 * tb + n
                    ins = nc.scalar.activation(square[:, :], mixed[:, tb, n * NC:(n + 1) * NC], ACT.Square,
                                               accum_out=stat[:, at:at + 1])
                    if n < NN - 1:
                        step(ins)
                    else:
                        ins.then_inc(squared, 1)
                        act.wait_ge(mean_ready, TB + 2 + 2 * TB + tb + 1)
                        nc.scalar.activation(stat[:, 8 + tb:9 + tb], stat[:, 4 + tb:5 + tb], ACT.Sqrt)\
                            .then_inc(root_ready, 1)

        @block.vector
        def _(dve):
            step = Steps(dve, dve_steps)

            def low(half, off):
                dve.wait_ge(hi_ready, 2 * half + off + 1)
                s = off % 2
                nc.vector.tensor_tensor(w_lo[:, s, :], w_raw[:, s, :], w_hi[:, s, :].bitcast(F32),
                                        ALU.subtract).then_inc(split_ready, 1)

            def turned_low(n, tb, q, bnk):
                dve.wait_ge(turned_hi, n + 1)
                at = (slice(None), slice(4 * q, 4 * q + 4), slice(tb * P, (tb + 1) * P))
                nc.vector.tensor_tensor(act_lo[at], bnk.rearrange("p (f t) -> p f t", f=4),
                                        act_hi[at].bitcast(F32), ALU.subtract).then_inc(turned_lo, 1)

            def mean(dst, src, n):
                nc.vector.tensor_scalar(dst, src, 1.0 / n, EPS, ALU.mult, ALU.add).then_inc(mean_ready, 1)

            low(0, 0)
            dve.wait_ge(gain0_loaded, 16)
            for tb in range(TB):
                one = slice(tb, tb + 1)
                dve.wait_ge(squared, tb + 1)
                mean(stat[:, 4 + tb:5 + tb], stat[:, one], D)
                dve.wait_ge(root_ready, tb + 1)
                step(nc.vector.reciprocal(stat[:, 12 + tb:13 + tb], stat[:, 8 + tb:9 + tb]))
                if tb >= 2:
                    dve.wait_ge(turned, KC * (tb - 1))
                nc.vector.scalar_tensor_tensor(out=x_norm[:, tb % 2, :], in0=x_in[:, tb % 2, :],
                                               scalar=stat[:, 12 + tb:13 + tb], in1=gain0[:, :],
                                               op0=ALU.mult, op1=ALU.mult).then_inc(normed, 1)
                for q in range(KC):
                    turned_low(KC * tb + q, tb, q, bank[(KC * tb + q) % 8])
            pos, neg = prm_all[:, :, PARAMS], prm_all[:, :, PARAMS + 1]
            dve.wait_ge(coef_ready, 1)
            step(nc.vector.tensor_tensor(pos, pos, neg, ALU.add))
            step(nc.vector.tensor_scalar(pos, pos, LRU_C, None, ALU.mult))
            nc.vector.tensor_scalar(neg, pos, -1.0, None, ALU.mult).then_inc(coef_ready, 1)
            dve.wait_ge(turned, KC * TB)
            step(nc.vector.memset(xs[:, 0:CONV - 1], 0.0))
            dve.wait_ge(consts_ready, 2)
            low(0, 1)
            low(0, 2)

            def y_low(ft):
                dve.wait_ge(y_hi, ft + 1)
                nc.vector.scalar_tensor_tensor(out=act_lo[:, ft, :], in0=y_raw[:, ft, :],
                                               scalar=ygain[:, ft:ft + 1],
                                               in1=act_hi[:, ft, :].bitcast(F32),
                                               op0=ALU.mult, op1=ALU.subtract).then_inc(y_lo, 1)

            PER_HEAD = 9

            def head_of(half, h0, u, last=False):
                h, off = h0 + u, 5 * u
                first = isinstance(h, int) and h == 0
                pr = prm[:, u, :]
                low(half, off + 3)
                low(half, off + 4)
                dve.wait_ge(soft_ready, h + 1)
                step(nc.vector.scalar_tensor_tensor(out=stick[:, :], in0=z_all[:, 0:SC], scalar=0.0,
                                                    in1=soft[:, :], op0=ALU.max, op1=ALU.add))
                nc.vector.tensor_tensor(stick[:, 0:512], stick[:, 0:512],
                                        later[:, :, :].rearrange("p a b -> p (a b)"), ALU.mult)\
                    .then_inc(stick_ready, 1)
                dve.wait_ge(v_turned, h + 1)
                nc.vector.tensor_copy(v_nat[:, :, :].rearrange("p a b -> p (a b)"), bank[6]).then_inc(v_ready, 1)
                low(half, off + 5)
                dve.wait_ge(x_out, h + 1)
                dve.wait_ge(params_ready, h + 1)
                step(nc.vector.tensor_scalar(xc[:, :], xs[:, 0:SEQ], pr[:, 0:1], pr[:, 4:5],
                                             ALU.mult, ALU.add))
                for k in range(1, CONV):
                    ins = nc.vector.scalar_tensor_tensor(out=xc[:, :], in0=xs[:, k:k + SEQ],
                                                         scalar=pr[:, k:k + 1], in1=xc[:, :],
                                                         op0=ALU.mult, op1=ALU.add)
                    if k < CONV - 1:
                        step(ins)
                    else:
                        ins.then_inc(xc_ready, 1)
                if last:
                    for ft in range(KC):
                        y_low(ft)
                dve.wait_ge(logw_ready, h + 1)
                if not first:
                    dve.wait_ge(av_ready, h)
                nc.vector.tensor_tensor(weight[:, 0:512], z_all[:, 0:512],
                                        never[:, :, :].rearrange("p a b -> p (a b)"), ALU.add)\
                    .then_inc(logd_ready, 1)
                low(half, off + 6)
                dve.wait_ge(av_ready, h + 1)
                if not first:
                    dve.wait_ge(ya_stored, h)
                nc.vector.tensor_copy(ya_t[:, :], bank[6]).then_inc(ya_ready, 1)
                if last:
                    for ft in range(KC, 2 * KC):
                        y_low(ft)
                low(half, off + 7)
                dve.wait_ge(ua_ready, 2 * h + 2)
                step(nc.vector.tensor_scalar(d_t[:, :], u_t[:, :], 1.0, None, ALU.add))
                step(nc.vector.reciprocal(d_t[:, :], d_t[:, :]))
                nc.vector.scalar_tensor_tensor(out=d_t[:, :], in0=u_t[:, :], scalar=2.0, in1=d_t[:, :],
                                               op0=ALU.mult, op1=ALU.mult).then_inc(v2_ready, 1)
                step(nc.vector.tensor_tensor(i_t[:, :], i_t[:, :], xc[:, :], ALU.mult))
                dve.wait_ge(mult_ready, h + 1)
                step(nc.vector.tensor_tensor(i_t[:, :], i_t[:, :], d_t[:, :], ALU.mult))
                step(nc.vector.tensor_tensor_scan(u_t[:, :], a_t[:, :], i_t[:, :], 0.0, ALU.mult, ALU.add))
                if not first:
                    dve.wait_ge(yl_stored, h)
                dve.wait_ge(g_out, h + 1)
                nc.vector.tensor_tensor(yl_t[:, :], u_t[:, :], gelu_t[:, :], ALU.mult).then_inc(yl_ready, 1)

            head_of(0, 0, 0)
            head_of(0, 0, 1)
            with dve.Fori(1, HEADS // 2 - 1) as t:
                step.loop(t, 1, 2 * PER_HEAD)
                head_of(5 * t, 2 * t, 0)
                head_of(5 * t, 2 * t, 1)
            step.end(HEADS // 2 - 2, 2 * PER_HEAD)
            t = HEADS // 2 - 1
            head_of(5 * t, 2 * t, 0)
            head_of(5 * t, 2 * t, 1, True)

            def row_stats(which):
                dve.wait_ge(ssq_ready, which + 1)
                mean(stat[:, 24 + 4 * which:28 + 4 * which], bank[0 if which else 3][:, 0:TB], HALF)
                dve.wait_ge(root_ready, TB + which + 1)
                nc.vector.reciprocal(stat[:, 32 + 4 * which:36 + 4 * which],
                                     stat[:, 16 + 4 * which:20 + 4 * which]).then_inc(rstd_ready, 1)

            def add_lru(n, tb):
                cols = slice(n * NC, (n + 1) * NC)
                dve.wait_ge(mix_a, TB * n + tb + 1)
                nc.vector.scalar_tensor_tensor(out=mixed[:, tb, cols], in0=SET_B[tb],
                                               scalar=stat[:, 36 + tb:37 + tb], in1=mixed[:, tb, cols],
                                               op0=ALU.mult, op1=ALU.add).then_inc(mix_b, 1)

            for n in range(NN):
                for kc in range(KC):
                    c = C_OUT + KC * n + kc
                    if c == C_OUT + KC:
                        dve.wait_ge(rstd_ready, 2)
                    if c + 1 >= C_OUT + 3:
                        low((c + 1) // 2, (c + 1) % 2)
                    if n == 0 and kc == 1:
                        row_stats(0)
                        for ft in range(2 * KC, 4 * KC):
                            y_low(ft)
                    if n == 0 and kc == 2:
                        row_stats(1)
                    if n >= 1 and kc == 0:
                        dve.wait_ge(chunk_used, c)
                        for tb in range(TB):
                            add_lru(n - 1, tb)
            dve.wait_ge(gains_loaded, 32)
            dve.wait_ge(resid_loaded, 16)
            for tb in range(TB):
                dve.wait_ge(last_out, tb + 1)
                add_lru(NN - 1, tb)
            for tb in range(TB):
                dve.wait_ge(squared, TB + 2 * tb + 1)
                step(nc.vector.reduce_sum(stat[:, tb:tb + 1], stat[:, 40 + 4 * tb:44 + 4 * tb], AX_X))
                mean(stat[:, 4 + tb:5 + tb], stat[:, tb:tb + 1], D)
                dve.wait_ge(root_ready, TB + 2 + 2 * tb + 1)
                step(nc.vector.reciprocal(stat[:, 12 + tb:13 + tb], stat[:, 8 + tb:9 + tb]))
                step(nc.vector.scalar_tensor_tensor(out=mixed[:, tb, :], in0=mixed[:, tb, :],
                                                    scalar=stat[:, 12 + tb:13 + tb], in1=gain1[:, :],
                                                    op0=ALU.mult, op1=ALU.mult))
                nc.vector.tensor_tensor(resid[:, tb, :], resid[:, tb, :], mixed[:, tb, :], ALU.add)\
                    .then_inc(resid_ready, 1)
                dve.wait_ge(squared, TB + 2 * tb + 2)
                mean(stat[:, 4 + tb:5 + tb], stat[:, tb:tb + 1], D)
                dve.wait_ge(root_ready, TB + 2 + 2 * tb + 2)
                step(nc.vector.reciprocal(stat[:, 12 + tb:13 + tb], stat[:, 8 + tb:9 + tb]))
                nc.vector.scalar_tensor_tensor(out=mixed[:, tb, :], in0=resid[:, tb, :],
                                               scalar=stat[:, 12 + tb:13 + tb], in1=gain2[:, :],
                                               op0=ALU.mult, op1=ALU.mult).then_inc(normed, 1)
                for q in range(KC):
                    turned_low(KC * (TB + tb) + q, tb, q, SET_A[q])
                if tb == 0:
                    low(C_FFN // 2, 1)

            def h_make(i, half, off):
                dve.wait_ge(silu_ready, KC * (i + 1))
                dve.wait_ge(chunk_used, 2 * half + off)
                for f in range(KC):
                    nc.vector.tensor_tensor(h_raw[:, f, :], SET_B[f], h_raw[:, f, :], ALU.mult)\
                        .then_inc(h_ready, 1)
                for f in range(KC):
                    dve.wait_ge(h_hi_ready, KC * i + f + 1)
                    nc.vector.tensor_tensor(h_lo[:, f, :], h_raw[:, f, :], h_hi[:, f, :].bitcast(F32),
                                            ALU.subtract).then_inc(h_lo_ready, 1)

            def add_down(half, off, n, banks, first, each=False):
                if not each:
                    dve.wait_ge(chunk_used, 2 * half + off)
                for tb in range(TB):
                    if each:
                        dve.wait_ge(last_out, TB + tb + 1)
                    to = mixed[:, tb, n * NC:(n + 1) * NC]
                    if first:
                        nc.vector.tensor_copy(to, banks[tb]).then_inc(down_out, 1)
                    else:
                        nc.vector.tensor_tensor(to, banks[tb], to, ALU.add).then_inc(down_out, 1)

            F = C_FFN // 2
            for kc in range(1, KC):
                low(F, kc + 1)
            for kc in range(KC):
                low(F, 4 + kc + 1)
            BABA = [SET_B, SET_A, SET_B, SET_A]

            def group(half, i, first=False):
                for kc in range(KC):
                    low(half, kc + 1)
                    if kc == 0:
                        h_make(i - 1, half, -1)
                for n in range(NN):
                    low(half, 4 + n + 1)
                    if n >= 1:
                        add_down(half, 4 + n - 1, n - 1, BABA[n - 1], first)
                for kc in range(KC):
                    low(half, 8 + kc + 1)
                    if kc == 0:
                        add_down(half, 7, 3, BABA[3], first)

            group(F + 4, 1, True)
            with dve.Fori(2, GROUPS) as i:
                group(F - 2 + 6 * i, i)
            half = (C_LAST - 4) // 2
            low(half, 1)
            h_make(GROUPS - 1, half, -1)
            low(half, 2)
            ABAB = [SET_A, SET_B, SET_A, SET_B]
            add_down(half, 0, 0, ABAB[0], False)
            low(half, 3)
            add_down(half, 1, 1, ABAB[1], False)
            add_down(half, 2, 2, ABAB[2], False)
            dve.wait_ge(gains_loaded, 48)
            add_down(half, 3, 3, ABAB[3], False, True)
            for tb in range(TB):
                dve.wait_ge(squared, 3 * TB + tb + 1)
                step(nc.vector.reduce_sum(stat[:, tb:tb + 1], stat[:, 40 + 4 * tb:44 + 4 * tb], AX_X))
                mean(stat[:, 4 + tb:5 + tb], stat[:, tb:tb + 1], D)
                dve.wait_ge(root_ready, 3 * TB + 2 + tb + 1)
                step(nc.vector.reciprocal(stat[:, 12 + tb:13 + tb], stat[:, 8 + tb:9 + tb]))
                step(nc.vector.scalar_tensor_tensor(out=mixed[:, tb, :], in0=mixed[:, tb, :],
                                                    scalar=stat[:, 12 + tb:13 + tb], in1=gain3[:, :],
                                                    op0=ALU.mult, op1=ALU.mult))
                nc.vector.tensor_tensor(mixed[:, tb, :], resid[:, tb, :], mixed[:, tb, :], ALU.add)\
                    .then_inc(final_ready, 1)

        @block.gpsimd
        def _(pool):
            step = Steps(pool, pool_steps)
            step(nc.gpsimd.memset(ident[:, :], 0.0))
            step(nc.gpsimd.memset(ones[:, :], 1.0))
            nc.gpsimd.affine_select(out=ident[:, :], in_=ident[:, :], compare_op=ALU.not_equal, fill=1.0,
                                    base=0, pattern=[[-1, P]], channel_multiplier=1).then_inc(consts_ready, 1)
            pool.wait_ge(turned, KC * TB)
            step(nc.gpsimd.memset(tri_neg[:, :], -1.0))
            step(nc.gpsimd.memset(ones_neg[:, :], -1.0))
            step(nc.gpsimd.memset(later[:, :, :], 1.0))
            step(nc.gpsimd.memset(never[:, :, :], 0.0))
            step(nc.gpsimd.memset(ssq[:, :, :], 0.0))
            step(nc.gpsimd.affine_select(out=tri_neg[:, :], in_=tri_neg[:, :], compare_op=ALU.is_ge, fill=0.0,
                                         base=0, pattern=[[-1, P]], channel_multiplier=1))
            step(nc.gpsimd.affine_select(out=later[:, :, :], in_=later[:, :, :], compare_op=ALU.is_gt,
                                         fill=0.0, base=0, pattern=[[0, 4], [1, P]], channel_multiplier=-1))
            nc.gpsimd.affine_select(out=never[:, :, :], in_=never[:, :, :], compare_op=ALU.is_gt,
                                    fill=NEVER, base=0, pattern=[[0, 4], [1, P]], channel_multiplier=-1)\
                .then_inc(consts_ready, 1)
            pool.wait_ge(coef_ready, 2)

            def store(h, which, src, done):
                at = y_raw[:, bass.ds(h + HEADS * which, 1), :].rearrange("p a n -> p (a n)")
                step(nc.gpsimd.tensor_copy(at, src))
                step(nc.gpsimd.tensor_tensor(sq_t[:, :], src, src, ALU.mult))
                nc.gpsimd.tensor_tensor(ssq[:, which, :], ssq[:, which, :], sq_t[:, :], ALU.add)\
                    .then_inc(done, 1)

            def params(h, u):
                nc.gpsimd.tensor_copy(prm[:, u, :], prm_all[:, bass.ds(h, 1), :]
                                      .rearrange("p a n -> p (a n)")).then_inc(params_ready, 1)

            def head_of(h, u, more):
                pool.wait_ge(ya_ready, h + 1)
                store(h, 0, ya_t[:, :], ya_stored)
                pool.wait_ge(yl_ready, h + 1)
                store(h, 1, yl_t[:, :], yl_stored)
                if more:
                    params(h + 2, u)

            params(0, 0)
            params(1, 1)
            with pool.Fori(0, HEADS // 2 - 1) as t:
                step.loop(t, 0, 8)
                head_of(2 * t, 0, True)
                head_of(2 * t + 1, 1, True)
            step.end(HEADS // 2 - 1, 8)
            head_of(HEADS - 2, 0, False)
            head_of(HEADS - 1, 1, False)


def kernel(x, pre_mix_norm, post_mix_norm, pre_ffn_norm, post_ffn_norm, w_in, conv_w, conv_b,
           w_rgate, b_rgate, w_igate, b_igate, lru_lambda, attn_out_norm, lru_out_norm, w_out,
           w_ffn_gate, w_ffn_up, w_ffn_down):
    import numpy as np
    import concourse.bacc as bacc
    from concourse.bass_utils import run_bass_kernel_spmd

    a = {k: np.asarray(v) for k, v in locals().items() if k not in ("np", "bacc", "run_bass_kernel_spmd")}
    seq, d = a["x"].shape[1:]
    params = np.concatenate([a["conv_w"][0], a["conv_b"], a["b_rgate"], a["b_igate"], a["lru_lambda"]])
    arrays = {
        "x_in_dram": a["x"].reshape(seq, d),
        "g_pre_mix": a["pre_mix_norm"].reshape(d),
        "g_post_mix": a["post_mix_norm"].reshape(d),
        "g_pre_ffn": a["pre_ffn_norm"].reshape(d),
        "g_post_ffn": a["post_ffn_norm"].reshape(d),
        "w_in_dram": a["w_in"][0],
        "lru_params": params.reshape(PARAMS, HEADS, P).transpose(2, 1, 0),
        "w_rgate_dram": a["w_rgate"][0],
        "w_igate_dram": a["w_igate"][0],
        "y_gains": np.concatenate([a["attn_out_norm"], a["lru_out_norm"]], 1).reshape(d // P, P).T,
        "w_out_dram": a["w_out"][0],
        "w_gate_dram": a["w_ffn_gate"][0],
        "w_up_dram": a["w_ffn_up"][0],
        "w_down_dram": a["w_ffn_down"][0],
    }
    arrays = {k: np.ascontiguousarray(v) for k, v in arrays.items()}
    nc = bacc.Bacc("TRN2", target_bir_lowering=False, num_devices=1)
    args = [nc.dram_tensor(k, v.shape, mybir.dt.from_np(v.dtype), kind="ExternalInput").ap()
            for k, v in arrays.items()]
    args.append(nc.dram_tensor("out_dram", (seq, d), F32, kind="ExternalOutput").ap())
    decoder_layer(nc, *args)
    got = run_bass_kernel_spmd(nc, [arrays], core_ids=[0])
    return got.results[0]["out_dram"].reshape(1, seq, d)
```

```python
from contextlib import ExitStack

import concourse.bass as bass
from concourse import mybir

F32 = mybir.dt.float32
F32R = mybir.dt.float32r
ALU = mybir.AluOpType
ACT = mybir.ActivationFunctionType
AX_X = mybir.AxisListType.X

P = 128
HEADS = 8
PARAMS = 8
EPS = 1e-6
LRU_C = 8.0
CONV = 4
NEVER = -1.0e30


class Steps:

    def __init__(self, engine, semaphore):
        self.engine, self.semaphore = engine, semaphore
        self.before, self.here = 0, 0

    def __call__(self, instruction):
        self.here += 1
        instruction.then_inc(self.semaphore, 1)
        self.engine.wait_ge(self.semaphore, self.before + self.here)

    def loop(self, index, first, per_pass):
        self.start = self.before + self.here
        self.before, self.here = index * per_pass + (self.start - first * per_pass), 0

    def end(self, passes, per_pass):
        assert self.here == per_pass, (self.here, per_pass)
        self.before, self.here = self.start + passes * per_pass, 0


def decoder_layer(nc, x, col_gains, g_post_mix, g_post_ffn, w_in, lru_params, w_rgate,
                  w_igate, w_out, w_gate, w_up, w_down, out):
    SEQ, D = x.shape
    TB = SEQ // P
    KT = D // P
    W = D // HEADS // 2
    HALF = D // 2
    NC = 512
    NN = D // NC
    KC = NC // P
    CH = KC * NC
    GROUPS = w_gate.shape[1] // NC
    SCALE = float(W) ** -0.5
    assert W == P and CH == KT * P and SEQ == 512 and KT == 16
    C_OUT = 5 * HEADS
    C_FFN = C_OUT + NN * (KT // KC)
    C_LAST = C_FFN + 12 * GROUPS
    OFF = {0: (512, 384), 2: (896, 128), 1: (1024, 256)}
    SC = 1280

    ctx = ExitStack()
    with ctx:
        def sb(name, shape, dt=F32, stack=ctx):
            return stack.enter_context(nc.sbuf_tensor(name, shape, dt))

        def sem(name):
            return ctx.enter_context(nc.semaphore(name))

        bank = [ctx.enter_context(nc.psum_tensor(f"bank{i}", [P, 512], F32)) for i in range(3)]
        scores3 = ctx.enter_context(nc.psum_tensor("scores3", [P, 3, 512], F32))
        bank += [scores3[:, i, :] for i in range(3)]
        bank += [ctx.enter_context(nc.psum_tensor(f"bank{i}", [P, 512], F32)) for i in (6, 7)]
        bank = [b[:, :] for b in bank]
        z_all = scores3[:, :, :].rearrange("p a b -> p (a b)")
        SET_A = [bank[i] for i in (0, 1, 2, 7)]
        SET_B = [bank[i] for i in (3, 4, 5, 6)]
        BABA, ABAB = [SET_B, SET_A] * 2, [SET_A, SET_B] * 2
        FIRST_KC = (0, 2, 1, 3)
        Y_ORDER = [KC * kc + k for kc in FIRST_KC for k in range(KC)]
        GATE_BANKS, LAST_GATE_BANKS = (3, 4), (7, 1)

        w_raw = sb("w_raw", [P, 2, CH])
        w_hi = sb("w_hi", [P, 2, CH], F32R)
        w_lo = sb("w_lo", [P, 2, CH], F32R)
        act_hi = sb("act_hi", [P, KT, SEQ], F32R)
        act_lo = sb("act_lo", [P, KT, SEQ], F32R)
        ident = sb("ident", [P, P])
        ones = sb("ones", [P, P])
        gains = sb("gains", [P, 3, KT])
        in_gain, y_gain, ffn_gain = (gains[:, n, :] for n in range(3))
        stat = sb("stat", [P, 64])
        sums = stat[:, 0:4 * TB].rearrange("p (t n) -> p t n", n=4)
        total, mean_sq, root, rstd = (stat[:, 16 + 4 * n:20 + 4 * n] for n in range(4))
        half_mean, half_root, half_rstd = ([stat[:, 32 + 8 * n + 4 * w:36 + 8 * n + 4 * w] for w in range(2)]
                                           for n in range(3))

        with ExitStack() as head:
            x_in = sb("x_in", [P, TB, D], stack=head)
            square0 = sb("square0", [P, 2, NC], stack=head)
            diag0 = sb("diag0", [P, TB, P], stack=head)
        with ExitStack() as mix:
            sb("over_x_in", [P, TB, D], stack=mix)
            sb("over_square0", [P, 2, NC], stack=mix)
            sb("over_diag0", [P, TB, P], stack=mix)
            row_scale = sb("row_scale", [P, SEQ], stack=mix)
        with ExitStack() as mix:
            y_raw = sb("y_raw", [P, KT, SEQ], stack=mix)
            ssq = sb("ssq", [P, 2, SEQ], stack=mix)
            sq_t = sb("sq_t", [P, SEQ], stack=mix)
            sb("over_row_scale", [P, SEQ], stack=mix)
            prm_all = sb("prm_all", [P, HEADS, PARAMS + 2], stack=mix)
            prm = sb("prm", [P, 2, PARAMS + 2], stack=mix)
            gate_w = sb("gate_w", [P, 2, 2, P], stack=mix)
            tri_neg = sb("tri_neg", [P, P], F32R, stack=mix)
            ones_neg = sb("ones_neg", [P, P], F32R, stack=mix)
            later = sb("later", [P, P], stack=mix)
            never = sb("never", [P, P], stack=mix)
            qk_t = sb("qk_t", [P, SEQ], stack=mix)
            q_hi = sb("q_hi", [P, SEQ], F32R, stack=mix)
            q_lo = sb("q_lo", [P, SEQ], F32R, stack=mix)
            k_hi = sb("k_hi", [P, SEQ], F32R, stack=mix)
            k_lo = sb("k_lo", [P, SEQ], F32R, stack=mix)
            vT = sb("vT", [P, SEQ], stack=mix)
            v_hi = sb("v_hi", [P, SEQ], F32R, stack=mix)
            v_lo = sb("v_lo", [P, SEQ], F32R, stack=mix)
            soft = sb("soft", [P, SC], stack=mix)
            soft_hi = sb("soft_hi", [P, SC], F32R, stack=mix)
            soft_lo = sb("soft_lo", [P, SC], F32R, stack=mix)
            xs = sb("xs", [P, CONV - 1 + SEQ], stack=mix)
            xc = sb("xc", [P, SEQ], stack=mix)
            made = xc[:, 0:2 * P].rearrange("p (a n) -> p a n", a=2)
            r_t = sb("r_t", [P, SEQ], stack=mix)
            i_t = sb("i_t", [P, SEQ], stack=mix)
            u_t = sb("u_t", [P, SEQ], stack=mix)
            a_t = sb("a_t", [P, SEQ], stack=mix)
            d_t = sb("d_t", [P, SEQ], stack=mix)
            gelu_t = sb("gelu_t", [P, SEQ], stack=mix)
            ya_t = sb("ya_t", [P, SEQ], stack=mix)
        with ExitStack() as tail:
            mixed = sb("mixed", [P, TB, D], stack=tail)
            resid = sb("resid", [P, TB, D], stack=tail)
            square = sb("square", [P, NC], stack=tail)
            row_scale2 = sb("row_scale2", [P, SEQ], stack=tail)
            with ExitStack() as mid:
                gain1 = sb("gain1", [P, D], stack=mid)
                diag2 = sb("diag2", [P, TB, P], stack=mid)
            with ExitStack() as ffn:
                h_hi = sb("h_hi", [P, KC, SEQ], F32R, stack=ffn)
                h_lo = sb("h_lo", [P, KC, SEQ], F32R, stack=ffn)
                h_raw = sb("h_raw", [P, KC, SEQ], stack=ffn)
            with ExitStack() as end:
                sb("over_h_hi", [P, KC, SEQ], F32R, stack=end)
                sb("over_h_lo", [P, KC, SEQ], F32R, stack=end)
                gain3 = sb("gain3", [P, D], stack=end)
        last_cols = w_raw[:, 0, :].rearrange("p (t n) -> p t n", t=TB)

        raw_loaded = [sem(f"raw_loaded{n}") for n in range(2)]
        hi_ready = sem("hi_ready")
        split_ready = sem("split_ready")
        chunk_used = sem("chunk_used")
        x_loaded = [sem(f"x_loaded{n}") for n in range(4)]
        gains_loaded = sem("gains_loaded")
        consts_ready = sem("consts_ready")
        coef_ready = sem("coef_ready")
        squared = sem("squared")
        mean_ready = sem("mean_ready")
        root_ready = sem("root_ready")
        rstd_ready = sem("rstd_ready")
        turned = sem("turned")
        turned_hi = sem("turned_hi")
        turned_lo = sem("turned_lo")
        diag_ready = sem("diag_ready")
        row_sums = sem("row_sums")
        row_scale_ready = sem("row_scale_ready")
        q_out = sem("q_out")
        q_hi_ready = sem("q_hi_ready")
        q_ready = sem("q_ready")
        k_out = sem("k_out")
        k_hi_ready = sem("k_hi_ready")
        k_ready = sem("k_ready")
        v_out = sem("v_out")
        v_turned = sem("v_turned")
        v_hi_ready = sem("v_hi_ready")
        v_ready = sem("v_ready")
        scores_ready = sem("scores_ready")
        smooth_ready = sem("smooth_ready")
        soft_ready = sem("soft_ready")
        stick_hi_ready = sem("stick_hi_ready")
        stick_ready = sem("stick_ready")
        logw_ready = sem("logw_ready")
        logd_ready = sem("logd_ready")
        weight_ready = sem("weight_ready")
        weight_hi_ready = sem("weight_hi_ready")
        weight_lo_ready = sem("weight_lo_ready")
        av_ready = sem("av_ready")
        ya_ready = sem("ya_ready")
        ya_stored = sem("ya_stored")
        params_ready = sem("params_ready")
        gate_w_loaded = [sem(f"gate_w_loaded{n}") for n in range(2)]
        x_out = sem("x_out")
        g_out = sem("g_out")
        xc_ready = sem("xc_ready")
        gates_ready = sem("gates_ready")
        ri_ready = sem("ri_ready")
        ua_ready = sem("ua_ready")
        v2_ready = sem("v2_ready")
        mult_ready = sem("mult_ready")
        gelu_ready = sem("gelu_ready")
        yl_ready = sem("yl_ready")
        yl_stored = sem("yl_stored")
        y_hi = sem("y_hi")
        y_lo = sem("y_lo")
        ssq_ready = sem("ssq_ready")
        mix_a = sem("mix_a")
        mix_b = sem("mix_b")
        mixed_squared = sem("mixed_squared")
        mixed_scaled = sem("mixed_scaled")
        last_out = sem("last_out")
        resid_loaded = sem("resid_loaded")
        gain1_loaded = sem("gain1_loaded")
        resid_ready = sem("resid_ready")
        early_tile = sem("early_tile")
        gate_scaled = sem("gate_scaled")
        silu_ready = sem("silu_ready")
        silu_scaled = sem("silu_scaled")
        h_made = sem("h_made")
        h_hi_ready = sem("h_hi_ready")
        h_lo_ready = sem("h_lo_ready")
        down_out = sem("down_out")
        gain3_loaded = sem("gain3_loaded")
        part_scaled = sem("part_scaled")
        block_scaled = sem("block_scaled")
        last_scaled = sem("last_scaled")
        stored = sem("stored")
        act_steps = sem("act_steps")
        dve_steps = sem("dve_steps")
        pool_steps = sem("pool_steps")
        final_ready = [sem(f"final_ready{n}") for n in range(4)]

        block = ctx.enter_context(nc.Block())

        def rows(w, r0, c0):
            return w[bass.ds(r0, NC), bass.ds(c0, NC)].rearrange("(k p) n -> p k n", p=P)

        def lead(c0):
            return w_in[:, bass.ds(c0, P)].rearrange("(k p) n -> p k n", p=P)

        @block.sync
        def _(sp):
            def load(half, off, src, k):
                if not (isinstance(half, int) and 2 * half + off < 2):
                    sp.wait_ge(split_ready, 2 * half + off - 1)
                dst = w_raw[:, off % 2, :].rearrange("p (k n) -> p k n", k=k)
                sp.dma_start(dst, src).then_inc(raw_loaded[off % 2], 16)

            def load_gates(h, slot):
                for n, w in enumerate((w_rgate, w_igate)):
                    sp.dma_start(gate_w[:, slot, n, :], w[bass.ds(h, 1)].rearrange("a c d -> (a c) d"))\
                        .then_inc(gate_w_loaded[slot], 16)

            x_rows = x.rearrange("(t p) d -> p t d", p=P)
            sp.dma_start(gains[:, :, :], col_gains).then_inc(gains_loaded, 16)
            sp.dma_start(prm_all[:, :, 0:PARAMS], lru_params).then_inc(gains_loaded, 16)
            for q in range(4):
                if q == 3:
                    load(0, 0, lead(0), KT)
                cols = slice(q * NC, (q + 1) * NC)
                sp.dma_start(x_in[:, :, cols], x_rows[:, :, cols]).then_inc(x_loaded[q], 16)
            load(0, 1, lead(HALF), KT)
            load_gates(0, 0)
            load_gates(1, 1)

            def head_pair(half, h0, last):
                for u in range(2):
                    h = h0 + u
                    for j in range(5):
                        off = 5 * u + 2 + j
                        if j < 3:
                            load(half, off, lead(h * P + (j + 2) * HALF), KT)
                        elif not (last and u == 1):
                            load(half, off, lead((h + 1) * P + (j - 3) * HALF), KT)
                        else:
                            load(half, off, rows(w_out, FIRST_KC[j - 3] * NC, 0), KC)
                        if j == 2 and not (isinstance(h, int) and h in (0, HEADS - 1)):
                            sp.wait_ge(gates_ready, h)
                            load_gates(h + 1, (u + 1) % 2)

            head_pair(0, 0, False)
            with sp.Fori(1, HEADS // 2 - 1) as t:
                head_pair(5 * t, 2 * t, False)
            head_pair(5 * (HEADS // 2 - 1), HEADS - 2, True)
            for c in range(C_OUT + 2, C_FFN):
                n, kc = divmod(c - C_OUT, KC)
                load(c // 2, c % 2, rows(w_out, (FIRST_KC[kc] if n == 0 else kc) * NC, n * NC), KC)
                if c >= C_OUT + 6 and c < C_OUT + 10:
                    q = c - C_OUT - 6
                    if q == 0:
                        sp.wait_ge(rstd_ready, 2)
                        sp.dma_start(gain1[:, :], g_post_mix.partition_broadcast(P)).then_inc(gain1_loaded, 16)
                    sp.dma_start(resid[:, q, :], x_rows[:, q, :]).then_inc(resid_loaded, 16)

            def load_in(half, off, w, i):
                for kc in range(KC):
                    load(half, off + kc, rows(w, kc * NC, i * NC), KC)

            def load_down(half, off, i):
                for n in range(NN):
                    load(half, off + n, rows(w_down, i * NC, n * NC), KC)

            load_in(C_FFN // 2, 0, w_gate, 0)
            load_in(C_FFN // 2, 4, w_up, 0)
            with sp.Fori(1, GROUPS) as i:
                half = C_FFN // 2 - 2 + 6 * i
                load_in(half, 0, w_gate, i)
                load_down(half, 4, i - 1)
                load_in(half, 8, w_up, i)
            load_down((C_LAST - 4) // 2, 0, GROUPS - 1)
            sp.wait_ge(h_lo_ready, KC * GROUPS)
            sp.dma_start(gain3[:, :], g_post_ffn.partition_broadcast(P)).then_inc(gain3_loaded, 16)
            for tb in range(TB):
                sp.wait_ge(final_ready[tb], 1)
                sp.dma_start(out[tb * P:(tb + 1) * P, :], mixed[:, tb, :]).then_inc(stored, 16)
            sp.wait_ge(stored, 16 * TB)

        @block.tensor
        def _(pe):
            def products(ps, lhs, rhs, start, stop, shared=False):
                (lh, ll), (rh, rl) = lhs, rhs
                pe.matmul(ps, lh, rh, start=start, stop=False, skip_group_check=shared)
                pe.matmul(ps, lh, rl, start=False, stop=False, skip_group_check=shared)
                return pe.matmul(ps, ll, rh, start=False, stop=stop, skip_group_check=shared)

            def column_tile(half, off, ps, first=False):
                pe.wait_ge(split_ready, 2 * half + off + 1)
                for kt in range(KT):
                    if first:
                        pe.wait_ge(turned_lo, max(kt, 8) + 1)
                    cols = slice(kt * P, (kt + 1) * P)
                    mm = products(ps, (w_hi[:, off % 2, cols], w_lo[:, off % 2, cols]),
                                  (act_hi[:, kt, :], act_lo[:, kt, :]), kt == 0, kt == KT - 1)
                mm.then_inc(chunk_used, 1)

            def turn(source, kt, bnk):
                for tb in range(TB):
                    mm = pe.transpose(bnk[:, tb * P:(tb + 1) * P], source[:, tb, kt * P:(kt + 1) * P],
                                      ident[:, :])
                mm.then_inc(turned, 1)

            pe.wait_ge(consts_ready, 1)
            for kt in range(KT):
                if kt % 4 == 0:
                    pe.wait_ge(x_loaded[kt // 4], 16)
                if kt >= 8:
                    pe.wait_ge(turned_lo, kt - 7)
                turn(x_in, kt, bank[kt % 8])

            def across(n, diag, bnk):
                pe.wait_ge(diag_ready, n + 1)
                pe.matmul(bnk, ones[:, :], diag[:, :, :].rearrange("p t n -> p (t n)"),
                          start=True, stop=True).then_inc(row_sums, 1)

            def diag(t, b):
                return t[:, b * P:(b + 1) * P]

            def scores(h):
                pe.wait_ge(q_ready, h + 1)
                pe.wait_ge(k_ready, h + 1)
                for b in range(TB):
                    products(diag(z_all, b), (diag(k_hi, b), diag(k_lo, b)), (diag(q_hi, b), diag(q_lo, b)),
                             b == 0, False, True)
                for b, (o, n) in OFF.items():
                    mm = products(z_all[:, o:o + n], (diag(k_hi, b), diag(k_lo, b)),
                                  (q_hi[:, SEQ - n:SEQ], q_lo[:, SEQ - n:SEQ]), b < 2, False, True)
                mm.then_inc(scores_ready, 1)

            def turn_v(h):
                pe.wait_ge(v_out, h + 1)
                if not (isinstance(h, int) and h == 0):
                    pe.wait_ge(ya_ready, h)
                for b in range(TB):
                    mm = pe.transpose(diag(bank[6], b), diag(vT, b), ident[:, :])
                mm.then_inc(v_turned, 1)

            def suffix(h):
                pe.wait_ge(stick_ready, h + 1)
                for kb in range(TB):
                    for jb in range(kb, TB):
                        lhs = (tri_neg if jb == kb else ones_neg)[:, :]
                        if jb == kb:
                            outs = [(diag(z_all, kb), diag, kb)]
                            if kb < TB - 1:
                                o, n = OFF[kb]
                                outs.append((z_all[:, o:o + n], None, (o, o + n)))
                        else:
                            o, n = OFF[kb]
                            at = o + (jb - kb - 1) * P
                            outs = [(z_all[:, at:at + P], diag, jb)]
                            if jb < TB - 1:
                                oj, nj = OFF[jb]
                                outs.append((z_all[:, at + P:o + n], None, (oj, oj + nj)))
                        for ps, block_of, at in outs:
                            for part in (soft_hi, soft_lo):
                                rhs = block_of(part, at) if block_of else part[:, at[0]:at[1]]
                                mm = pe.matmul(ps, lhs, rhs, start=False,
                                               stop=(kb == TB - 1 and part is soft_lo),
                                               skip_group_check=True)
                mm.then_inc(logw_ready, 1)

            def attend(h):
                pe.wait_ge(v_ready, h + 1)
                pe.wait_ge(weight_lo_ready, h + 1)
                for b in range(TB):
                    v_b = (diag(v_hi, b), diag(v_lo, b))
                    mm = products(diag(bank[6], b), v_b, (diag(soft_hi, b), diag(soft_lo, b)), b == 0,
                                  b == TB - 1, True)
                    if b < TB - 1:
                        o, n = OFF[b]
                        products(bank[6][:, SEQ - n:SEQ], v_b, (soft_hi[:, o:o + n], soft_lo[:, o:o + n]),
                                 False, False, True)
                mm.then_inc(av_ready, 1)

            def gates(h, turn_no, slot, banks=GATE_BANKS):
                pe.wait_ge(xc_ready, h + 1)
                pe.wait_ge(gate_w_loaded[slot], 32 * turn_no)
                for n in range(2):
                    mm = pe.matmul(bank[banks[n]], gate_w[:, slot, n, :], xc[:, :], start=True, stop=True)
                mm.then_inc(gates_ready, 1)

            def head_of(half, h0, t, u, last=False):
                h, off = h0 + u, 5 * u
                first = isinstance(h, int) and h == 0
                if not first:
                    pe.wait_ge(x_out, h)
                column_tile(half, off + 1, bank[1])
                pe.wait_ge(q_out, h + 1)
                column_tile(half, off + 2, bank[0])
                if not first:
                    pe.wait_ge(ri_ready, 2 * h)
                scores(h)
                pe.wait_ge(k_out, h + 1)
                column_tile(half, off + 3, bank[1])
                turn_v(h)
                if not first:
                    pe.wait_ge(g_out, h)
                column_tile(half, off + 4, bank[2])
                if last:
                    pe.wait_ge(x_out, h + 1)
                    gates(h, t + 1, u, LAST_GATE_BANKS)
                suffix(h)
                if not last:
                    pe.wait_ge(v_out, h + 1)
                    column_tile(half, off + 5, bank[0])
                    attend(h)
                    gates(h, t + 1, u)

            column_tile(0, 0, bank[0], True)
            across(0, diag0, bank[7])
            pe.wait_ge(consts_ready, 2)
            head_of(0, 0, 0, 0)
            head_of(0, 0, 0, 1)
            with pe.Fori(1, HEADS // 2 - 1) as t:
                head_of(5 * t, 2 * t, t, 0)
                head_of(5 * t, 2 * t, t, 1)
            t = HEADS // 2 - 1
            head_of(5 * t, 2 * t, t, 0)
            head_of(5 * t, 2 * t, t, 1, True)

            def row_blocks(half, off, lhs, k0, banks, start, stop, free=None, inputs=None, sem_each=None):
                pe.wait_ge(split_ready, 2 * half + off + 1)
                for tb in range(TB):
                    if free is not None:
                        free(tb)
                    for k in range(KC):
                        if inputs is not None and tb == 0:
                            inputs(k)
                        toks = slice(tb * P, (tb + 1) * P)
                        cols = slice(k * NC, (k + 1) * NC)
                        mm = products(banks[tb], (lhs[0][:, k0 + k, toks], lhs[1][:, k0 + k, toks]),
                                      (w_hi[:, off % 2, cols], w_lo[:, off % 2, cols]),
                                      start and k == 0, stop and k == KC - 1)
                    if sem_each is not None:
                        mm.then_inc(sem_each, 1)
                if sem_each is None:
                    mm.then_inc(chunk_used, 1)

            def token_sums(which, bnk):
                pe.wait_ge((ya_stored, yl_stored)[which], HEADS)
                for tb in range(TB):
                    mm = pe.matmul(bnk[:, tb:tb + 1], ssq[:, which, tb * P:(tb + 1) * P], ones[:, 0:1],
                                   start=(tb == 0), stop=(tb == TB - 1), skip_group_check=True)
                mm.then_inc(ssq_ready, 1)

            def free_first(tb, c):
                if c == 0:
                    if tb == 1:
                        pe.wait_ge(ri_ready, 2 * HEADS)
                    if tb == 2:
                        pe.wait_ge(g_out, HEADS)
                elif c == 1:
                    if tb == 3:
                        pe.wait_ge(ya_ready, HEADS)
                        token_sums(0, bank[6])
                        pe.wait_ge(mean_ready, 2)
                elif c == KC:
                    pe.wait_ge(mix_a, tb + 1)
                    if tb == 3:
                        token_sums(1, bank[7])
                        pe.wait_ge(mean_ready, 3)

            for n in range(NN):
                for j in range(KC):
                    c = C_OUT + KC * n + j
                    kc = FIRST_KC[j] if n == 0 else j

                    def free(tb, n=n, kc=kc, c=c):
                        if c - C_OUT in (0, 1, KC):
                            free_first(tb, c - C_OUT)
                        elif kc % 2 == 0:
                            pe.wait_ge(mix_a if kc == 0 else mix_b, TB * (n - 1) + tb + 1)

                    def inputs(k, n=n, j=j):
                        if n == 0:
                            pe.wait_ge(y_lo, KC * j + k + 1)
                    row_blocks(c // 2, c % 2, (act_hi, act_lo), KC * kc, SET_A if kc < 2 else SET_B,
                               kc % 2 == 0, kc % 2 == 1, free, inputs, last_out if c == C_FFN - 1 else None)
                    if j == 0 and n == 0:
                        attend(HEADS - 1)

            def into_ffn(half, off, banks, kcs, early=False):
                for kc in kcs:
                    pe.wait_ge(split_ready, 2 * half + off + kc + 1)
                    slot = (off + kc) % 2
                    for f in range(KC):
                        for k in range(KC):
                            at = k * NC + f * P
                            mm = products(banks[f], (w_hi[:, slot, at:at + P], w_lo[:, slot, at:at + P]),
                                          (act_hi[:, KC * kc + k, :], act_lo[:, KC * kc + k, :]),
                                          kc == k == 0, kc == k == KC - 1)
                        if early and kc == KC - 1 and f < KC - 1:
                            mm.then_inc(early_tile, 1)
                    mm.then_inc(chunk_used, 1)

            def turn_quarter(q):
                for k in range(4):
                    kt = 4 * q + k
                    pe.wait_ge(resid_ready, TB * (q + 1))
                    if q >= 1:
                        pe.wait_ge(turned_lo, KT + kt - 3)
                    turn(resid, kt, SET_B[k])

            F = C_FFN // 2
            pe.wait_ge(mix_b, TB * NN)
            turn_quarter(0)
            turn_quarter(1)
            for kc in range(KC):
                pe.wait_ge(turned_lo, KT + 4 * kc + 4)
                if kc == 0:
                    pe.wait_ge(mix_a, TB * NN)
                into_ffn(F, 0, SET_A, [kc])
                if kc < 2:
                    turn_quarter(kc + 2)
                if kc == 2:
                    pe.wait_ge(turned_lo, 2 * KT)
                    across(1, diag2, SET_B[0])
            pe.wait_ge(row_scale_ready, 1)
            into_ffn(F, 4, SET_B, range(KC), True)

            def down(half, off, i, sets, free, is_last=False):
                for n in range(NN):
                    free(n)
                    row_blocks(half, off + n, (h_hi, h_lo), 0, sets[n], True, True,
                               inputs=(lambda k: pe.wait_ge(h_lo_ready, KC * i + k + 1)) if n == 0 else None,
                               sem_each=last_out if is_last and n == NN - 1 else None)

            def group(half, i, first=False):
                if first:
                    pe.wait_ge(gate_scaled, KC)
                else:
                    pe.wait_ge(down_out, TB * NN * (i - 1))
                into_ffn(half, 0, SET_A, range(KC))

                def free(n):
                    if n == 0:
                        pe.wait_ge(h_made, KC * i)
                    if n == 1:
                        pe.wait_ge(gate_scaled, KC * (i + 1))
                    if n >= 2:
                        pe.wait_ge(down_out, TB * NN * (i - 1) + TB * (n - 1))
                down(half, 4, i - 1, BABA, free)
                pe.wait_ge(down_out, TB * NN * (i - 1) + TB * 3)
                into_ffn(half, 8, SET_B, range(KC), True)

            group(F + 4, 1, True)
            with pe.Fori(2, GROUPS) as i:
                group(F - 2 + 6 * i, i)

            def free(n):
                if n == 0:
                    pe.wait_ge(down_out, TB * NN * (GROUPS - 1))
                if n == 1:
                    pe.wait_ge(h_made, KC * GROUPS)
                if n >= 2:
                    pe.wait_ge(down_out, TB * NN * (GROUPS - 1) + TB * (n - 1))
            down((C_LAST - 4) // 2, 0, GROUPS - 1, ABAB, free, True)

        def until_used(engine, half, off, after_w_out=False):
            if isinstance(half, int):
                c = 2 * half + off
                if c == C_FFN - 1:
                    engine.wait_ge(last_out, TB)
                else:
                    engine.wait_ge(chunk_used, c + 1 - (c >= C_FFN))
            else:
                engine.wait_ge(chunk_used, 2 * half + off + (0 if after_w_out else 1))

        def y_source(ft):
            return gelu_t[:, :] if ft == KT - 1 else y_raw[:, ft, :]

        @block.scalar
        def _(act):
            step = Steps(act, act_steps)

            def high(half, off, kc=None, in_ffn=False):
                act.wait_ge(raw_loaded[off % 2], 16 * (half + off // 2 + 1))
                if not (isinstance(half, int) and 2 * half + off < 2):
                    until_used(act, half, off - 2, in_ffn)
                if kc is None:
                    nc.scalar.activation(w_hi[:, off % 2, :], w_raw[:, off % 2, :], ACT.Copy)\
                        .then_inc(hi_ready, 1)
                    return
                for k in range(KC):
                    cols, row = slice(k * NC, (k + 1) * NC), KC * kc + k
                    ins = nc.scalar.activation(w_hi[:, off % 2, cols], w_raw[:, off % 2, cols], ACT.Copy,
                                               scale=ffn_gain[:, row:row + 1])
                ins.then_inc(hi_ready, 1)

            def copy_high(dst, src, done, **scale):
                nc.scalar.activation(dst, src, ACT.Copy, **scale).then_inc(done, 1)

            def take_root(n):
                act.wait_ge(mean_ready, n)
                nc.scalar.activation(root, mean_sq, ACT.Sqrt).then_inc(root_ready, 1)

            act.wait_ge(gains_loaded, 32)
            lam = prm_all[:, :, PARAMS - 1]
            pos, neg = prm_all[:, :, PARAMS], prm_all[:, :, PARAMS + 1]
            step(nc.scalar.activation(pos, lam, ACT.Abs))
            step(nc.scalar.activation(pos, pos, ACT.Exp, scale=-1.0))
            step(nc.scalar.activation(pos, pos, ACT.Ln, bias=1.0))
            nc.scalar.activation(neg, lam, ACT.Relu, scale=-1.0).then_inc(coef_ready, 1)
            for kt in range(KT):
                act.wait_ge(turned, kt + 1)
                copy_high(act_hi[:, kt, :], bank[kt % 8], turned_hi, scale=in_gain[:, kt:kt + 1])
                if kt == 11:
                    high(0, 0)
            for q in range(4):
                for tb in range(2):
                    step(nc.scalar.activation(square0[:, 0, :], x_in[:, tb, q * NC:(q + 1) * NC], ACT.Square,
                                              accum_out=sums[:, tb, q:q + 1]))
            high(0, 1)
            take_root(1)
            act.wait_ge(consts_ready, 2)
            copy_high(tri_neg[:, :], made[:, 0, :], coef_ready)
            copy_high(ones_neg[:, :], made[:, 1, :], coef_ready)

            def q_high(h):
                if not (isinstance(h, int) and h == 0):
                    act.wait_ge(scores_ready, h)
                act.wait_ge(q_out, h + 1)
                copy_high(q_hi[:, :], qk_t[:, :], q_hi_ready)

            def y_high(n):
                ft = Y_ORDER[n]
                if ft == KT - 1:
                    act.wait_ge(yl_ready, HEADS)
                else:
                    act.wait_ge(ya_stored if ft < HEADS else yl_stored, ft % HEADS + 1)
                copy_high(act_hi[:, ft, :], y_source(ft), y_hi, scale=y_gain[:, ft:ft + 1])

            def gate_values(h, u, banks=GATE_BANKS):
                act.wait_ge(gates_ready, h + 1)
                act.wait_ge(params_ready, h + 1)
                nc.scalar.activation(r_t[:, :], bank[banks[0]], ACT.Sigmoid, bias=prm[:, u, 5:6])\
                    .then_inc(ri_ready, 1)
                nc.scalar.activation(i_t[:, :], bank[banks[1]], ACT.Sigmoid, bias=prm[:, u, 6:7])\
                    .then_inc(ri_ready, 1)

            def decay(h, u):
                act.wait_ge(ri_ready, 2 * h + 2)
                nc.scalar.activation(u_t[:, :], r_t[:, :], ACT.Tanh, scale=prm[:, u, 8:9]).then_inc(ua_ready, 1)
                nc.scalar.activation(a_t[:, :], r_t[:, :], ACT.Exp, scale=prm[:, u, 9:10]).then_inc(ua_ready, 1)
                act.wait_ge(v2_ready, h + 1)
                nc.scalar.activation(d_t[:, :], d_t[:, :], ACT.Sqrt).then_inc(mult_ready, 1)

            PER_HEAD = 2

            def head_of(half, h0, u, last=False):
                h, off = h0 + u, 5 * u
                first = isinstance(h, int) and h == 0
                high(half, off + 3)
                act.wait_ge(k_out, h + 1)
                if not first:
                    act.wait_ge(scores_ready, h)
                copy_high(k_hi[:, :], qk_t[:, :], k_hi_ready)
                high(half, off + 4)
                act.wait_ge(scores_ready, h + 1)
                if not first:
                    act.wait_ge(weight_lo_ready, h)
                step(nc.scalar.activation(soft[:, :], z_all[:, 0:SC], ACT.Abs))
                step(nc.scalar.activation(soft[:, :], soft[:, :], ACT.Exp, scale=-1.0))
                nc.scalar.activation(soft[:, :], soft[:, :], ACT.Ln, bias=1.0).then_inc(smooth_ready, 1)
                act.wait_ge(v_turned, h + 1)
                if not first:
                    act.wait_ge(av_ready, h)
                copy_high(v_hi[:, :], bank[6], v_hi_ready)
                high(half, off + 5)
                act.wait_ge(soft_ready, h + 1)
                copy_high(soft_hi[:, :], soft[:, :], stick_hi_ready)
                if last:
                    until_used(act, half, off + 4)
                    for n in range(KC):
                        y_high(n)
                    gate_values(h, u, LAST_GATE_BANKS)
                high(half, off + 6)
                act.wait_ge(logw_ready, h + 1)
                act.wait_ge(stick_ready, h + 1)
                nc.scalar.activation(soft[:, 512:SC], z_all[:, 512:SC], ACT.Exp).then_inc(weight_ready, 1)
                act.wait_ge(logd_ready, h + 1)
                nc.scalar.activation(soft[:, 0:512], soft[:, 0:512], ACT.Exp).then_inc(weight_ready, 1)
                act.wait_ge(weight_ready, 2 * h + 2)
                copy_high(soft_hi[:, :], soft[:, :], weight_hi_ready)
                act.wait_ge(g_out, h + 1)
                nc.scalar.activation(gelu_t[:, :], gelu_t[:, :], ACT.Gelu_apprx_tanh).then_inc(gelu_ready, 1)
                if not last:
                    high(half, off + 7)
                    q_high(h + 1)
                    gate_values(h, u)
                else:
                    for n in range(KC, 2 * KC):
                        y_high(n)
                    high(half, off + 7)
                    for n in range(2 * KC, 3 * KC):
                        y_high(n)
                decay(h, u)

            q_high(0)
            high(0, 2)
            head_of(0, 0, 0)
            head_of(0, 0, 1)
            with act.Fori(1, HEADS // 2 - 1) as t:
                step.loop(t, 1, 2 * PER_HEAD)
                head_of(5 * t, 2 * t, 0)
                head_of(5 * t, 2 * t, 1)
            step.end(HEADS // 2 - 2, 2 * PER_HEAD)
            t = HEADS // 2 - 1
            head_of(5 * t, 2 * t, 0)
            head_of(5 * t, 2 * t, 1, True)

            def half_roots(which):
                act.wait_ge(mean_ready, which + 2)
                nc.scalar.activation(half_root[which], half_mean[which], ACT.Sqrt).then_inc(root_ready, 1)

            def square_of(tb, n, made_before, before, source=None):
                act.wait_ge(*made_before)
                if before + TB * n + tb > 0:
                    act.wait_ge(mixed_squared, before + TB * n + tb)
                if source is None:
                    source = mixed[:, tb, n * NC:(n + 1) * NC]
                nc.scalar.activation(square[:, :], source, ACT.Square,
                                     accum_out=sums[:, tb, n:n + 1]).then_inc(mixed_squared, 1)

            def root_of(tb, before):
                act.wait_ge(mixed_squared, before + TB * (NN - 1) + tb + 1)
                nc.scalar.activation(root[:, tb:tb + 1], sums[:, tb, NN - 1:NN], ACT.Sqrt, scale=1.0 / D,
                                     bias=mean_sq[:, tb:tb + 1]).then_inc(root_ready, 1)

            half_roots(0)
            for n in range(3 * KC, 4 * KC):
                y_high(n)
            F = C_FFN // 2
            for c in range(C_OUT + 2, C_FFN):
                n, j = divmod(c - C_OUT, KC)
                high((c + 1) // 2, (c + 1) % 2, 0 if c + 1 == C_FFN else None)
                if j == (3 if n == 0 else 2):
                    until_used(act, (c - 1) // 2, (c - 1) % 2)
                    act.wait_ge(rstd_ready, 1)
                    act.wait_ge(y_lo, KT)
                    for tb in range(TB):
                        nc.scalar.activation(mixed[:, tb, n * NC:(n + 1) * NC], SET_A[tb], ACT.Copy,
                                             scale=half_rstd[0][:, tb:tb + 1]).then_inc(mix_a, 1)
                if n == 1 and j == 0:
                    half_roots(1)
                if n >= 1 and j == 1:
                    for tb in range(TB):
                        square_of(tb, n - 1, (mix_b, TB * (n - 1) + tb + 1), 0)
            act.wait_ge(mean_ready, 4)
            for tb in range(TB):
                square_of(tb, NN - 1, (mix_b, TB * (NN - 1) + tb + 1), 0)
                root_of(tb, 0)
            high(F, 1, 1)

            def turned_high(q):
                for kt in range(4 * q, 4 * q + 4):
                    act.wait_ge(turned, KT + kt + 1)
                    copy_high(act_hi[:, kt, :], SET_B[kt % 4], turned_hi)

            turned_high(0)
            turned_high(1)
            turned_high(2)
            high(F, 2, 2)
            act.wait_ge(resid_ready, TB * 4)
            for tb in range(TB):
                nc.scalar.activation(mixed[:, tb, :], resid[:, tb, :], ACT.Square,
                                     accum_out=total[:, tb:tb + 1]).then_inc(squared, 1)
            take_root(5)
            turned_high(3)
            high(F, 3, 3)

            def silu(i):
                for f in range(KC):
                    act.wait_ge(gate_scaled, KC * i + f + 1)
                    nc.scalar.activation(h_raw[:, f, :], h_raw[:, f, :], ACT.Silu).then_inc(silu_ready, 1)

            def h_high(i):
                for f in range(KC):
                    act.wait_ge(h_made, KC * i + f + 1)
                    copy_high(h_hi[:, f, :], h_raw[:, f, :], h_hi_ready)

            high(F, 4, 0)
            high(F, 5, 1)
            silu(0)
            high(F, 6, 2)
            high(F, 7, 3)
            high(F, 8, 0)
            h_high(0)

            def group(half, i, last=False):
                for c in range(12):
                    nxt = c + 1
                    kc = nxt % 4 if nxt < 4 or nxt >= 8 else None
                    if nxt == 12:
                        kc = None if last else 0
                    high(half, nxt, kc, True)
                    if c == 4:
                        silu(i)
                h_high(i)

            with act.Fori(1, GROUPS - 1) as i:
                group(F - 2 + 6 * i, i)
            half = F - 2 + 6 * (GROUPS - 1)
            group(half, GROUPS - 1, True)
            before = TB * NN * (GROUPS - 1)
            for n in range(NN):
                if n < NN - 1:
                    high(half, 13 + n)
                for tb in range(TB):
                    square_of(tb, n, (down_out, before + TB * n + tb + 1), TB * NN,
                              last_cols[:, tb, :] if n == NN - 1 else None)
                    if n == NN - 1:
                        act.wait_ge(mean_ready, 6)
                        root_of(tb, TB * NN)
                    if n == NN - 1 and tb == 1:
                        act.wait_ge(part_scaled, TB * (NN - 1))
                        act.wait_ge(last_scaled, 1)
                        act.wait_ge(rstd_ready, 3)
                        nc.scalar.activation(mixed[:, 0, :], mixed[:, 0, :], ACT.Copy,
                                             scale=rstd[:, 0:1]).then_inc(block_scaled, 1)

        @block.vector
        def _(dve):
            step = Steps(dve, dve_steps)
            SUB = ALU.subtract

            def low(half, off, kc=None):
                dve.wait_ge(hi_ready, 2 * half + off + 1)
                s = off % 2
                if kc is None:
                    nc.vector.tensor_tensor(w_lo[:, s, :], w_raw[:, s, :], w_hi[:, s, :].bitcast(F32), SUB)\
                        .then_inc(split_ready, 1)
                    return
                for k in range(KC):
                    cols, row = slice(k * NC, (k + 1) * NC), KC * kc + k
                    ins = nc.vector.scalar_tensor_tensor(
                        out=w_lo[:, s, cols], in0=w_raw[:, s, cols], scalar=ffn_gain[:, row:row + 1],
                        in1=w_hi[:, s, cols].bitcast(F32), op0=ALU.mult, op1=SUB)
                ins.then_inc(split_ready, 1)

            def rest(dst, src, high_part, done):
                nc.vector.tensor_tensor(dst, src, high_part.bitcast(F32), SUB).then_inc(done, 1)

            def mean(dst, src, n):
                nc.vector.tensor_scalar(dst, src, 1.0 / n, EPS, ALU.mult, ALU.add).then_inc(mean_ready, 1)

            def diagonal(diag, n):
                dve.wait_ge(root_ready, n)
                step(nc.vector.reciprocal(rstd, root))
                for tb in range(TB):
                    ins = nc.vector.tensor_scalar(diag[:, tb, :], ident[:, :], rstd[:, tb:tb + 1], None,
                                                  ALU.mult)
                ins.then_inc(diag_ready, 1)

            dve.wait_ge(consts_ready, 1)
            dve.wait_ge(gains_loaded, 32)
            for kt in range(KT):
                dve.wait_ge(turned_hi, kt + 1)
                nc.vector.scalar_tensor_tensor(out=act_lo[:, kt, :], in0=bank[kt % 8],
                                               scalar=in_gain[:, kt:kt + 1],
                                               in1=act_hi[:, kt, :].bitcast(F32),
                                               op0=ALU.mult, op1=SUB).then_inc(turned_lo, 1)
                if kt == 11:
                    low(0, 0)
            for q in range(4):
                for tb in range(2, TB):
                    part = x_in[:, tb, q * NC:(q + 1) * NC]
                    step(nc.vector.tensor_tensor_reduce(out=square0[:, 1, :], in0=part, in1=part, scale=1.0,
                                                        scalar=0.0, op0=ALU.mult, op1=ALU.add,
                                                        accum_out=sums[:, tb, q:q + 1]))
            dve.wait_ge(act_steps, 11)
            step(nc.vector.reduce_sum(total, sums, AX_X))
            mean(mean_sq, total, D)
            diagonal(diag0, 1)
            low(0, 1)
            dve.wait_ge(row_sums, 1)
            step(nc.vector.tensor_copy(row_scale[:, :], bank[7]))

            def scaled_out(dst, bnk, done):
                nc.vector.tensor_tensor(dst, bnk, row_scale[:, :], ALU.mult).then_inc(done, 1)

            def q_scaled(half, off):
                until_used(dve, half, off)
                nc.vector.scalar_tensor_tensor(out=qk_t[:, :], in0=bank[0], scalar=SCALE,
                                               in1=row_scale[:, :], op0=ALU.mult, op1=ALU.mult)\
                    .then_inc(q_out, 1)

            def q_low(h):
                dve.wait_ge(q_hi_ready, h + 1)
                rest(q_lo[:, :], qk_t[:, :], q_hi[:, :], q_ready)

            def y_low(n):
                ft = Y_ORDER[n]
                dve.wait_ge(y_hi, n + 1)
                nc.vector.scalar_tensor_tensor(out=act_lo[:, ft, :], in0=y_source(ft),
                                               scalar=y_gain[:, ft:ft + 1],
                                               in1=act_hi[:, ft, :].bitcast(F32),
                                               op0=ALU.mult, op1=SUB).then_inc(y_lo, 1)

            def half_mean_of(which, bnk):
                dve.wait_ge(ssq_ready, which + 1)
                mean(half_mean[which], bnk[:, 0:TB], HALF)

            def half_scale(which):
                dve.wait_ge(root_ready, which + 2)
                nc.vector.reciprocal(half_rstd[which], half_root[which]).then_inc(rstd_ready, 1)

            q_scaled(0, 0)
            pos, neg = prm_all[:, :, PARAMS], prm_all[:, :, PARAMS + 1]
            dve.wait_ge(coef_ready, 1)
            step(nc.vector.tensor_tensor(pos, pos, neg, ALU.add))
            step(nc.vector.tensor_scalar(pos, pos, LRU_C, None, ALU.mult))
            nc.vector.tensor_scalar(neg, pos, -1.0, None, ALU.mult).then_inc(coef_ready, 1)
            step(nc.vector.memset(xs[:, 0:CONV - 1], 0.0))
            dve.wait_ge(consts_ready, 2)
            q_low(0)
            low(0, 2)
            PER_HEAD = 9

            def head_of(half, h0, u, last=False):
                h, off = h0 + u, 5 * u
                first = isinstance(h, int) and h == 0
                pr = prm[:, u, :]
                until_used(dve, half, off + 1)
                dve.wait_ge(q_ready, h + 1)
                scaled_out(qk_t[:, :], bank[1], k_out)
                low(half, off + 3)
                dve.wait_ge(k_hi_ready, h + 1)
                rest(k_lo[:, :], qk_t[:, :], k_hi[:, :], k_ready)
                until_used(dve, half, off + 2)
                if not first:
                    dve.wait_ge(v_turned, h)
                scaled_out(vT[:, :], bank[0], v_out)
                low(half, off + 4)
                dve.wait_ge(smooth_ready, h + 1)
                step(nc.vector.scalar_tensor_tensor(out=soft[:, :], in0=z_all[:, 0:SC], scalar=0.0,
                                                    in1=soft[:, :], op0=ALU.max, op1=ALU.add))
                soft_d = soft[:, 0:512].rearrange("p (b t) -> p b t", b=TB)
                nc.vector.tensor_tensor(soft_d, soft_d, later[:, :].unsqueeze(1).broadcast_to([P, TB, P]),
                                        ALU.mult).then_inc(soft_ready, 1)
                dve.wait_ge(v_hi_ready, h + 1)
                rest(v_lo[:, :], bank[6], v_hi[:, :], v_ready)
                until_used(dve, half, off + 3)
                scaled_out(xs[:, CONV - 1:CONV - 1 + SEQ], bank[1], x_out)
                low(half, off + 5)
                dve.wait_ge(stick_hi_ready, h + 1)
                rest(soft_lo[:, :], soft[:, :], soft_hi[:, :], stick_ready)
                dve.wait_ge(x_out, h + 1)
                dve.wait_ge(params_ready, h + 1)
                step(nc.vector.tensor_scalar(xc[:, :], xs[:, 0:SEQ], pr[:, 0:1], pr[:, 4:5],
                                             ALU.mult, ALU.add))
                for k in range(1, CONV):
                    ins = nc.vector.scalar_tensor_tensor(out=xc[:, :], in0=xs[:, k:k + SEQ],
                                                         scalar=pr[:, k:k + 1], in1=xc[:, :],
                                                         op0=ALU.mult, op1=ALU.add)
                    if k < CONV - 1:
                        step(ins)
                    else:
                        ins.then_inc(xc_ready, 1)
                until_used(dve, half, off + 4)
                if not first:
                    dve.wait_ge(yl_stored, h)
                scaled_out(gelu_t[:, :], bank[2], g_out)
                if last:
                    for n in range(KC):
                        y_low(n)
                low(half, off + 6)
                dve.wait_ge(logw_ready, h + 1)
                nc.vector.tensor_tensor(soft_d, z_all[:, 0:512].rearrange("p (b t) -> p b t", b=TB),
                                        never[:, :].unsqueeze(1).broadcast_to([P, TB, P]), ALU.add)\
                    .then_inc(logd_ready, 1)
                dve.wait_ge(weight_hi_ready, h + 1)
                rest(soft_lo[:, :], soft[:, :], soft_hi[:, :], weight_lo_ready)
                if not last:
                    dve.wait_ge(k_ready, h + 1)
                    q_scaled(half, off + 5)
                    low(half, off + 7)
                    q_low(h + 1)
                else:
                    for n in range(KC, 2 * KC):
                        y_low(n)
                    low(half, off + 7)
                dve.wait_ge(av_ready, h + 1)
                if not first:
                    dve.wait_ge(ya_stored, h)
                nc.vector.tensor_copy(ya_t[:, :], bank[6]).then_inc(ya_ready, 1)
                if last:
                    half_mean_of(0, bank[6])
                    for n in range(2 * KC, 3 * KC):
                        y_low(n)
                dve.wait_ge(ua_ready, 2 * h + 2)
                step(nc.vector.tensor_scalar(d_t[:, :], u_t[:, :], 1.0, None, ALU.add))
                step(nc.vector.reciprocal(d_t[:, :], d_t[:, :]))
                nc.vector.scalar_tensor_tensor(out=d_t[:, :], in0=u_t[:, :], scalar=2.0, in1=d_t[:, :],
                                               op0=ALU.mult, op1=ALU.mult).then_inc(v2_ready, 1)
                step(nc.vector.tensor_tensor(i_t[:, :], i_t[:, :], xc[:, :], ALU.mult))
                dve.wait_ge(mult_ready, h + 1)
                step(nc.vector.tensor_tensor(i_t[:, :], i_t[:, :], d_t[:, :], ALU.mult))
                step(nc.vector.tensor_tensor_scan(u_t[:, :], a_t[:, :], i_t[:, :], 0.0, ALU.mult, ALU.add))
                dve.wait_ge(gelu_ready, h + 1)
                nc.vector.tensor_tensor(gelu_t[:, :], u_t[:, :], gelu_t[:, :], ALU.mult).then_inc(yl_ready, 1)

            head_of(0, 0, 0)
            head_of(0, 0, 1)
            with dve.Fori(1, HEADS // 2 - 1) as t:
                step.loop(t, 1, 2 * PER_HEAD)
                head_of(5 * t, 2 * t, 0)
                head_of(5 * t, 2 * t, 1)
            step.end(HEADS // 2 - 2, 2 * PER_HEAD)
            t = HEADS // 2 - 1
            head_of(5 * t, 2 * t, 0)
            head_of(5 * t, 2 * t, 1, True)

            def mean_but_last(count):
                dve.wait_ge(mixed_squared, count)
                step(nc.vector.reduce_sum(total, sums[:, :, 0:NN - 1], AX_X))
                mean(mean_sq, total, D)

            def add_lru(n, tb):
                cols = slice(n * NC, (n + 1) * NC)
                dve.wait_ge(mix_a, TB * n + tb + 1)
                nc.vector.scalar_tensor_tensor(out=mixed[:, tb, cols], in0=SET_B[tb],
                                               scalar=half_rstd[1][:, tb:tb + 1], in1=mixed[:, tb, cols],
                                               op0=ALU.mult, op1=ALU.add).then_inc(mix_b, 1)

            half_scale(0)
            for n in range(3 * KC, 4 * KC):
                y_low(n)
            F = C_FFN // 2
            for c in range(C_OUT + 2, C_FFN):
                n, j = divmod(c - C_OUT, KC)
                low((c + 1) // 2, (c + 1) % 2, 0 if c + 1 == C_FFN else None)
                if n == 1 and j == 0:
                    half_mean_of(1, bank[7])
                    half_scale(1)
                    dve.wait_ge(rstd_ready, 2)
                if n >= 1 and j == 0:
                    until_used(dve, (c - 1) // 2, (c - 1) % 2)
                    for tb in range(TB):
                        add_lru(n - 1, tb)
                if c == C_FFN - 2:
                    mean_but_last(TB * (NN - 1))
            for tb in range(TB):
                dve.wait_ge(last_out, tb + 1)
                add_lru(NN - 1, tb)
            dve.wait_ge(root_ready, 7)
            step(nc.vector.reciprocal(rstd, root))
            dve.wait_ge(resid_loaded, 16 * TB)

            def add_mixed(q):
                cols = slice(q * NC, (q + 1) * NC)
                dve.wait_ge(mixed_scaled, TB * (q + 1))
                for tb in range(TB):
                    nc.vector.scalar_tensor_tensor(out=resid[:, tb, cols], in0=mixed[:, tb, cols],
                                                   scalar=rstd[:, tb:tb + 1], in1=resid[:, tb, cols],
                                                   op0=ALU.mult, op1=ALU.add).then_inc(resid_ready, 1)

            def turned_rest(q):
                for kt in range(4 * q, 4 * q + 4):
                    dve.wait_ge(turned_hi, KT + kt + 1)
                    rest(act_lo[:, kt, :], SET_B[kt % 4], act_hi[:, kt, :], turned_lo)

            add_mixed(0)
            add_mixed(1)
            turned_rest(0)
            low(F, 1, 1)
            add_mixed(2)
            turned_rest(1)
            add_mixed(3)
            turned_rest(2)
            low(F, 2, 2)
            dve.wait_ge(squared, TB)
            mean(mean_sq, total, D)
            diagonal(diag2, 8)
            turned_rest(3)
            low(F, 3, 3)
            dve.wait_ge(row_sums, 2)
            nc.vector.tensor_copy(row_scale2[:, :], SET_B[0]).then_inc(row_scale_ready, 1)

            def gate_out(i, half, off):
                until_used(dve, half, off, True)
                for f in range(KC):
                    nc.vector.tensor_tensor(h_raw[:, f, :], SET_A[f], row_scale2[:, :], ALU.mult)\
                        .then_inc(gate_scaled, 1)

            def h_make(i, half, off):
                dve.wait_ge(silu_scaled, KC * (i + 1))
                for f in range(KC):
                    if f < KC - 1:
                        dve.wait_ge(early_tile, (KC - 1) * i + f + 1)
                    else:
                        until_used(dve, half, off, True)
                    nc.vector.tensor_tensor(h_raw[:, f, :], SET_B[f], h_raw[:, f, :], ALU.mult)\
                        .then_inc(h_made, 1)
                    dve.wait_ge(h_hi_ready, KC * i + f + 1)
                    rest(h_lo[:, f, :], h_raw[:, f, :], h_hi[:, f, :], h_lo_ready)

            def add_down(half, off, n, banks, first=False):
                until_used(dve, half, off, True)
                for tb in range(TB):
                    to = mixed[:, tb, n * NC:(n + 1) * NC]
                    if first:
                        nc.vector.tensor_copy(to, banks[tb]).then_inc(down_out, 1)
                    else:
                        nc.vector.tensor_tensor(to, banks[tb], to, ALU.add).then_inc(down_out, 1)

            low(F, 4, 0)
            dve.wait_ge(row_scale_ready, 1)
            gate_out(0, F, 3)
            low(F, 5, 1)
            low(F, 6, 2)
            low(F, 7, 3)
            low(F, 8, 0)
            h_make(0, F, 7)

            def group(half, i, first=False, last=False):
                for c in range(12):
                    nxt = c + 1
                    kc = nxt % 4 if nxt < 4 or nxt >= 8 else None
                    if nxt == 12:
                        kc = None if last else 0
                    if c == 4:
                        gate_out(i, half, 3)
                    low(half, nxt, kc)
                    if 5 <= c <= 8:
                        add_down(half, c - 1, c - 5, BABA[c - 5], first)
                h_make(i, half, 11)

            group(F + 4, 1, True)
            with dve.Fori(2, GROUPS - 1) as i:
                group(F - 2 + 6 * i, i)
            half = F - 2 + 6 * (GROUPS - 1)
            group(half, GROUPS - 1, False, True)
            for n in range(NN - 1):
                low(half, 13 + n)
                add_down(half, 12 + n, n, ABAB[n])

            def last_sum(tb):
                dve.wait_ge(last_out, TB + tb + 1)
                nc.vector.tensor_tensor(last_cols[:, tb, :], ABAB[NN - 1][tb],
                                        mixed[:, tb, (NN - 1) * NC:NN * NC], ALU.add).then_inc(down_out, 1)

            def last_rstd(tb):
                dve.wait_ge(root_ready, 9 + tb)
                nc.vector.reciprocal(rstd[:, tb:tb + 1], root[:, tb:tb + 1]).then_inc(rstd_ready, 1)

            def add_resid(tb):
                dve.wait_ge(rstd_ready, 3 + tb)
                dve.wait_ge(part_scaled, TB * (NN - 1))
                dve.wait_ge(last_scaled, tb + 1)
                nc.vector.scalar_tensor_tensor(out=mixed[:, tb, :], in0=mixed[:, tb, :],
                                               scalar=rstd[:, tb:tb + 1], in1=resid[:, tb, :],
                                               op0=ALU.mult, op1=ALU.add).then_inc(final_ready[tb], 1)

            last_sum(0)
            mean_but_last(2 * TB * NN - TB)
            last_rstd(0)
            last_sum(1)
            last_rstd(1)
            last_sum(2)
            add_resid(1)
            last_sum(3)
            last_rstd(2)
            add_resid(2)
            last_rstd(3)
            add_resid(3)

        @block.gpsimd
        def _(pool):
            step = Steps(pool, pool_steps)
            step(nc.gpsimd.memset(ident[:, :], 0.0))
            step(nc.gpsimd.memset(ones[:, :], 1.0))
            nc.gpsimd.affine_select(out=ident[:, :], in_=ident[:, :], compare_op=ALU.not_equal, fill=1.0,
                                    base=0, pattern=[[-1, P]], channel_multiplier=1).then_inc(consts_ready, 1)
            step(nc.gpsimd.memset(made, -1.0))
            step(nc.gpsimd.memset(later[:, :], 1.0))
            step(nc.gpsimd.memset(never[:, :], 0.0))
            step(nc.gpsimd.affine_select(out=made[:, 0, :], in_=made[:, 0, :], compare_op=ALU.is_ge, fill=0.0,
                                         base=0, pattern=[[-1, P]], channel_multiplier=1))
            step(nc.gpsimd.affine_select(out=later[:, :], in_=later[:, :], compare_op=ALU.is_gt,
                                         fill=0.0, base=0, pattern=[[1, P]], channel_multiplier=-1))
            nc.gpsimd.affine_select(out=never[:, :], in_=never[:, :], compare_op=ALU.is_gt,
                                    fill=NEVER, base=0, pattern=[[1, P]], channel_multiplier=-1)\
                .then_inc(consts_ready, 1)
            pool.wait_ge(row_sums, 1)
            step(nc.gpsimd.memset(ssq[:, :, :], 0.0))
            pool.wait_ge(coef_ready, 4)

            def store(h, which, src, done):
                at = y_raw[:, bass.ds(h + HEADS * which, 1), :].rearrange("p a n -> p (a n)")
                step(nc.gpsimd.tensor_copy(at, src))
                step(nc.gpsimd.tensor_tensor(sq_t[:, :], src, src, ALU.mult))
                nc.gpsimd.tensor_tensor(ssq[:, which, :], ssq[:, which, :], sq_t[:, :], ALU.add)\
                    .then_inc(done, 1)

            def params(h, u):
                nc.gpsimd.tensor_copy(prm[:, u, :], prm_all[:, bass.ds(h, 1), :]
                                      .rearrange("p a n -> p (a n)")).then_inc(params_ready, 1)

            def head_of(h, u, more):
                pool.wait_ge(ya_ready, h + 1)
                store(h, 0, ya_t[:, :], ya_stored)
                pool.wait_ge(yl_ready, h + 1)
                store(h, 1, gelu_t[:, :], yl_stored)
                if more:
                    params(h + 2, u)

            params(0, 0)
            params(1, 1)
            with pool.Fori(0, HEADS // 2 - 1) as t:
                step.loop(t, 0, 8)
                head_of(2 * t, 0, True)
                head_of(2 * t + 1, 1, True)
            step.end(HEADS // 2 - 1, 8)
            head_of(HEADS - 2, 0, False)
            head_of(HEADS - 1, 1, False)

            def scale_parts(gain, before, parts, done):
                for n in range(parts):
                    for tb in range(TB):
                        cols = slice(n * NC, (n + 1) * NC)
                        pool.wait_ge(mixed_squared, before + TB * n + tb + 1)
                        nc.gpsimd.tensor_tensor(mixed[:, tb, cols], mixed[:, tb, cols], gain[:, cols],
                                                ALU.mult).then_inc(done, 1)

            pool.wait_ge(gain1_loaded, 16)
            scale_parts(gain1, 0, NN, mixed_scaled)
            pool.wait_ge(row_scale_ready, 1)

            def scale_silu(i):
                for f in range(KC):
                    pool.wait_ge(silu_ready, KC * i + f + 1)
                    nc.gpsimd.tensor_tensor(h_raw[:, f, :], h_raw[:, f, :], row_scale2[:, :], ALU.mult)\
                        .then_inc(silu_scaled, 1)

            with pool.Fori(0, GROUPS) as i:
                scale_silu(i)
            pool.wait_ge(gain3_loaded, 16)
            scale_parts(gain3, TB * NN, NN - 1, part_scaled)
            for tb in range(TB):
                pool.wait_ge(down_out, TB * NN * GROUPS - TB + tb + 1)
                nc.gpsimd.tensor_tensor(mixed[:, tb, (NN - 1) * NC:NN * NC], last_cols[:, tb, :],
                                        gain3[:, (NN - 1) * NC:NN * NC], ALU.mult).then_inc(last_scaled, 1)
                if tb == 1:
                    pool.wait_ge(block_scaled, 1)
                    nc.gpsimd.tensor_tensor(mixed[:, 0, :], mixed[:, 0, :], resid[:, 0, :], ALU.add)\
                        .then_inc(final_ready[0], 1)

def kernel(x, pre_mix_norm, post_mix_norm, pre_ffn_norm, post_ffn_norm, w_in, conv_w, conv_b,
           w_rgate, b_rgate, w_igate, b_igate, lru_lambda, attn_out_norm, lru_out_norm, w_out,
           w_ffn_gate, w_ffn_up, w_ffn_down):
    import numpy as np
    import concourse.bacc as bacc
    from concourse.bass_utils import run_bass_kernel_spmd

    a = {k: np.asarray(v) for k, v in locals().items() if k not in ("np", "bacc", "run_bass_kernel_spmd")}
    seq, d = a["x"].shape[1:]
    params = np.concatenate([a["conv_w"][0], a["conv_b"], a["b_rgate"], a["b_igate"], a["lru_lambda"]])
    col_gains = np.concatenate([a["pre_mix_norm"], a["attn_out_norm"], a["lru_out_norm"],
                                a["pre_ffn_norm"]], 1)
    arrays = {
        "x_in_dram": a["x"].reshape(seq, d),
        "col_gains": col_gains.reshape(3, d // P, P).transpose(2, 0, 1),
        "g_post_mix": a["post_mix_norm"].reshape(d),
        "g_post_ffn": a["post_ffn_norm"].reshape(d),
        "w_in_dram": a["w_in"][0],
        "lru_params": params.reshape(PARAMS, HEADS, P).transpose(2, 1, 0),
        "w_rgate_dram": a["w_rgate"][0],
        "w_igate_dram": a["w_igate"][0],
        "w_out_dram": a["w_out"][0],
        "w_gate_dram": a["w_ffn_gate"][0],
        "w_up_dram": a["w_ffn_up"][0],
        "w_down_dram": a["w_ffn_down"][0],
    }
    arrays = {k: np.ascontiguousarray(v) for k, v in arrays.items()}
    nc = bacc.Bacc("TRN2", target_bir_lowering=False, num_devices=1)
    args = [nc.dram_tensor(k, v.shape, mybir.dt.from_np(v.dtype), kind="ExternalInput").ap()
            for k, v in arrays.items()]
    args.append(nc.dram_tensor("out_dram", (seq, d), F32, kind="ExternalOutput").ap())
    decoder_layer(nc, *args)
    got = run_bass_kernel_spmd(nc, [arrays], core_ids=[0])
    return got.results[0]["out_dram"].reshape(1, seq, d)
```

```python
from contextlib import ExitStack

import concourse.bass as bass
from concourse import mybir

F32 = mybir.dt.float32
F32R = mybir.dt.float32r
ALU = mybir.AluOpType
ACT = mybir.ActivationFunctionType
AX_X = mybir.AxisListType.X

P = 128
HEADS = 8
PARAMS = 8
EPS = 1e-6
LRU_C = 8.0
CONV = 4
NEVER = -1.0e30


class Steps:

    def __init__(self, engine, semaphore):
        self.engine, self.semaphore = engine, semaphore
        self.before, self.here = 0, 0

    def __call__(self, instruction):
        self.here += 1
        instruction.then_inc(self.semaphore, 1)
        self.engine.wait_ge(self.semaphore, self.before + self.here)

    def loop(self, index, first, per_pass):
        self.start = self.before + self.here
        self.before, self.here = index * per_pass + (self.start - first * per_pass), 0

    def end(self, passes, per_pass):
        assert self.here == per_pass, (self.here, per_pass)
        self.before, self.here = self.start + passes * per_pass, 0


def decoder_layer(nc, x, col_gains, g_post_mix, g_post_ffn, w_in, lru_params, w_rgate,
                  w_igate, w_out, w_gate, w_up, w_down, out):
    SEQ, D = x.shape
    TB = SEQ // P
    KT = D // P
    W = D // HEADS // 2
    HALF = D // 2
    NC = 512
    NN = D // NC
    KC = NC // P
    CH = KC * NC
    GROUPS = w_gate.shape[1] // NC
    SCALE = float(W) ** -0.5
    assert W == P and CH == KT * P and SEQ == 512 and KT == 16
    C_OUT = 5 * HEADS
    C_FFN = C_OUT + NN * (KT // KC)
    C_LAST = C_FFN + 12 * GROUPS
    ROW = {0: (0, 512), 1: (512, 384), 2: (1024, 256), 3: (896, 128)}
    SC = 1280

    ctx = ExitStack()
    with ctx:
        def sb(name, shape, dt=F32, stack=ctx):
            return stack.enter_context(nc.sbuf_tensor(name, shape, dt))

        def sem(name):
            return ctx.enter_context(nc.semaphore(name))

        bank = [ctx.enter_context(nc.psum_tensor(f"bank{i}", [P, 512], F32)) for i in range(3)]
        scores3 = ctx.enter_context(nc.psum_tensor("scores3", [P, 3, 512], F32))
        bank += [scores3[:, i, :] for i in range(3)]
        bank += [ctx.enter_context(nc.psum_tensor(f"bank{i}", [P, 512], F32)) for i in (6, 7)]
        bank = [b[:, :] for b in bank]
        z_all = scores3[:, :, :].rearrange("p a b -> p (a b)")
        SET_A = [bank[i] for i in (0, 1, 2, 7)]
        SET_B = [bank[i] for i in (3, 4, 5, 6)]
        BABA, ABAB = [SET_B, SET_A] * 2, [SET_A, SET_B] * 2
        FIRST_KC = (0, 2, 1, 3)
        Y_ORDER = [KC * kc + k for kc in FIRST_KC for k in range(KC)]
        GATE_BANKS, LAST_GATE_BANKS = (3, 4), (7, 1)
        LAST_BLOCKS = [(2, 0), (2, 1), (3, 0), (3, 1), (2, 2), (3, 2), (2, 3), (3, 3)]
        HALVES = [slice(0, D // 2), slice(D // 2, D)]

        w_raw = sb("w_raw", [P, 2, CH])
        w_hi = sb("w_hi", [P, 2, CH], F32R)
        w_lo = sb("w_lo", [P, 2, CH], F32R)
        act_hi = sb("act_hi", [P, KT, SEQ], F32R)
        act_lo = sb("act_lo", [P, KT, SEQ], F32R)
        ident = sb("ident", [P, P])
        ones = sb("ones", [P, P])
        gains = sb("gains", [P, 3, KT])
        in_gain, y_gain, ffn_gain = (gains[:, n, :] for n in range(3))
        stat = sb("stat", [P, 64])
        sums = stat[:, 0:4 * TB].rearrange("p (t n) -> p t n", n=4)
        total, mean_sq, root, rstd = (stat[:, 16 + 4 * n:20 + 4 * n] for n in range(4))
        half_mean, half_root, half_rstd = ([stat[:, 32 + 8 * n + 4 * w:36 + 8 * n + 4 * w] for w in range(2)]
                                           for n in range(3))

        with ExitStack() as head:
            x_in = sb("x_in", [P, TB, D], stack=head)
            square0 = sb("square0", [P, 2, NC], stack=head)
            diag0 = sb("diag0", [P, TB, P], stack=head)
        with ExitStack() as mix:
            sb("over_x_in", [P, TB, D], stack=mix)
            sb("over_square0", [P, 2, NC], stack=mix)
            sb("over_diag0", [P, TB, P], stack=mix)
            row_scale = sb("row_scale", [P, SEQ], stack=mix)
        with ExitStack() as mix:
            y_raw = sb("y_raw", [P, KT, SEQ], stack=mix)
            ssq = sb("ssq", [P, 2, SEQ], stack=mix)
            sq_t = sb("sq_t", [P, SEQ], stack=mix)
            sb("over_row_scale", [P, SEQ], stack=mix)
            prm_all = sb("prm_all", [P, HEADS, PARAMS + 2], stack=mix)
            prm = sb("prm", [P, 2, PARAMS + 2], stack=mix)
            gate_w = sb("gate_w", [P, 2, 2, P], stack=mix)
            tri_neg = sb("tri_neg", [P, P], F32R, stack=mix)
            ones_neg = sb("ones_neg", [P, P], F32R, stack=mix)
            later = sb("later", [P, P], stack=mix)
            never = sb("never", [P, P], stack=mix)
            qk_t = sb("qk_t", [P, SEQ], stack=mix)
            q_hi = sb("q_hi", [P, SEQ], F32R, stack=mix)
            q_lo = sb("q_lo", [P, SEQ], F32R, stack=mix)
            k_hi = sb("k_hi", [P, SEQ], F32R, stack=mix)
            k_lo = sb("k_lo", [P, SEQ], F32R, stack=mix)
            vT = sb("vT", [P, SEQ], stack=mix)
            v_hi = sb("v_hi", [P, SEQ], F32R, stack=mix)
            v_lo = sb("v_lo", [P, SEQ], F32R, stack=mix)
            soft = sb("soft", [P, SC], stack=mix)
            soft_hi = sb("soft_hi", [P, SC], F32R, stack=mix)
            soft_lo = sb("soft_lo", [P, SC], F32R, stack=mix)
            xs = sb("xs", [P, CONV - 1 + SEQ], stack=mix)
            xc = sb("xc", [P, SEQ], stack=mix)
            made = xc[:, 0:2 * P].rearrange("p (a n) -> p a n", a=2)
            r_t = sb("r_t", [P, SEQ], stack=mix)
            i_t = sb("i_t", [P, SEQ], stack=mix)
            u_t = sb("u_t", [P, SEQ], stack=mix)
            a_t = sb("a_t", [P, SEQ], stack=mix)
            d_t = sb("d_t", [P, SEQ], stack=mix)
            gelu_t = sb("gelu_t", [P, SEQ], stack=mix)
            ya_t = sb("ya_t", [P, SEQ], stack=mix)
        with ExitStack() as tail:
            mixed = sb("mixed", [P, TB, D], stack=tail)
            resid = sb("resid", [P, TB, D], stack=tail)
            square = sb("square", [P, NC], stack=tail)
            row_scale2 = sb("row_scale2", [P, SEQ], stack=tail)
            with ExitStack() as mid:
                gain1 = sb("gain1", [P, D], stack=mid)
                diag2 = sb("diag2", [P, TB, P], stack=mid)
            with ExitStack() as ffn:
                h_hi = sb("h_hi", [P, KC, SEQ], F32R, stack=ffn)
                h_lo = sb("h_lo", [P, KC, SEQ], F32R, stack=ffn)
                h_raw = sb("h_raw", [P, KC, SEQ], stack=ffn)
            with ExitStack() as end:
                sb("over_h_hi", [P, KC, SEQ], F32R, stack=end)
                sb("over_h_lo", [P, KC, SEQ], F32R, stack=end)
                gain3 = sb("gain3", [P, D], stack=end)
        last_cols = w_raw[:, 0, :].rearrange("p (t n) -> p t n", t=TB)

        raw_loaded = [sem(f"raw_loaded{n}") for n in range(2)]
        hi_ready = sem("hi_ready")
        split_ready = sem("split_ready")
        chunk_used = sem("chunk_used")
        x_loaded = [sem(f"x_loaded{n}") for n in range(4)]
        gains_loaded = sem("gains_loaded")
        consts_ready = sem("consts_ready")
        coef_ready = sem("coef_ready")
        squared = sem("squared")
        mean_ready = sem("mean_ready")
        root_ready = sem("root_ready")
        rstd_ready = sem("rstd_ready")
        turned = sem("turned")
        turned_hi = sem("turned_hi")
        turned_lo = sem("turned_lo")
        diag_ready = sem("diag_ready")
        row_sums = sem("row_sums")
        row_scale_ready = sem("row_scale_ready")
        q_out = sem("q_out")
        q_hi_ready = sem("q_hi_ready")
        q_ready = sem("q_ready")
        k_out = sem("k_out")
        k_hi_ready = sem("k_hi_ready")
        k_ready = sem("k_ready")
        v_out = sem("v_out")
        v_turned = sem("v_turned")
        v_hi_ready = sem("v_hi_ready")
        v_ready = sem("v_ready")
        scores_ready = sem("scores_ready")
        smooth_ready = sem("smooth_ready")
        soft_ready = sem("soft_ready")
        stick_hi_ready = sem("stick_hi_ready")
        stick_ready = sem("stick_ready")
        logw_ready = sem("logw_ready")
        logd_ready = sem("logd_ready")
        weight_ready = sem("weight_ready")
        weight_hi_ready = sem("weight_hi_ready")
        weight_lo_ready = sem("weight_lo_ready")
        av_ready = sem("av_ready")
        ya_ready = sem("ya_ready")
        ya_stored = sem("ya_stored")
        params_ready = sem("params_ready")
        gate_w_loaded = [sem(f"gate_w_loaded{n}") for n in range(2)]
        x_out = sem("x_out")
        g_out = sem("g_out")
        xc_ready = sem("xc_ready")
        gates_ready = sem("gates_ready")
        ri_ready = sem("ri_ready")
        ua_ready = sem("ua_ready")
        v2_ready = sem("v2_ready")
        mult_ready = sem("mult_ready")
        gelu_ready = sem("gelu_ready")
        yl_ready = sem("yl_ready")
        yl_stored = sem("yl_stored")
        y_hi = sem("y_hi")
        y_lo = sem("y_lo")
        ssq_made = sem("ssq_made")
        ssq_ready = sem("ssq_ready")
        mix_a = sem("mix_a")
        mix_b = sem("mix_b")
        mixed_squared = sem("mixed_squared")
        mixed_scaled = sem("mixed_scaled")
        last_out = sem("last_out")
        resid_loaded = sem("resid_loaded")
        gain1_loaded = sem("gain1_loaded")
        resid_ready = sem("resid_ready")
        early_tile = sem("early_tile")
        gate_scaled = sem("gate_scaled")
        silu_ready = sem("silu_ready")
        silu_scaled = sem("silu_scaled")
        h_made = sem("h_made")
        h_hi_ready = sem("h_hi_ready")
        h_lo_ready = sem("h_lo_ready")
        down_out = sem("down_out")
        gain3_loaded = sem("gain3_loaded")
        last_scaled = sem("last_scaled")
        stored = sem("stored")
        act_steps = sem("act_steps")
        dve_steps = sem("dve_steps")
        pool_steps = sem("pool_steps")
        final_ready = [sem(f"final_ready{n}") for n in range(4)]

        block = ctx.enter_context(nc.Block())

        def rows(w, r0, c0):
            return w[bass.ds(r0, NC), bass.ds(c0, NC)].rearrange("(k p) n -> p k n", p=P)

        def lead(c0):
            return w_in[:, bass.ds(c0, P)].rearrange("(k p) n -> p k n", p=P)

        @block.sync
        def _(sp):
            def load(half, off, src, k):
                if not (isinstance(half, int) and 2 * half + off < 2):
                    sp.wait_ge(split_ready, 2 * half + off - 1)
                dst = w_raw[:, off % 2, :].rearrange("p (k n) -> p k n", k=k)
                sp.dma_start(dst, src).then_inc(raw_loaded[off % 2], 16)

            def load_gates(h, slot):
                for n, w in enumerate((w_rgate, w_igate)):
                    sp.dma_start(gate_w[:, slot, n, :], w[bass.ds(h, 1)].rearrange("a c d -> (a c) d"))\
                        .then_inc(gate_w_loaded[slot], 16)

            x_rows = x.rearrange("(t p) d -> p t d", p=P)
            sp.dma_start(gains[:, :, :], col_gains).then_inc(gains_loaded, 16)
            sp.dma_start(prm_all[:, :, 0:PARAMS], lru_params).then_inc(gains_loaded, 16)
            for q in range(4):
                if q == 2:
                    load(0, 0, lead(0), KT)
                cols = slice(q * NC, (q + 1) * NC)
                sp.dma_start(x_in[:, :, cols], x_rows[:, :, cols]).then_inc(x_loaded[q], 16)
            load(0, 1, lead(HALF), KT)
            load_gates(0, 0)
            load_gates(1, 1)

            def head_pair(half, h0, last):
                for u in range(2):
                    h = h0 + u
                    for j in range(5):
                        off = 5 * u + 2 + j
                        if j < 3:
                            load(half, off, lead(h * P + (j + 2) * HALF), KT)
                        elif not (last and u == 1):
                            load(half, off, lead((h + 1) * P + (j - 3) * HALF), KT)
                        else:
                            load(half, off, rows(w_out, FIRST_KC[j - 3] * NC, 0), KC)
                        if j == 2 and not (isinstance(h, int) and h in (0, HEADS - 1)):
                            sp.wait_ge(gates_ready, h)
                            load_gates(h + 1, (u + 1) % 2)

            head_pair(0, 0, False)
            with sp.Fori(1, HEADS // 2 - 1) as t:
                head_pair(5 * t, 2 * t, False)
            head_pair(5 * (HEADS // 2 - 1), HEADS - 2, True)
            for c in range(C_OUT + 2, C_FFN):
                n, kc = divmod(c - C_OUT, KC)
                load(c // 2, c % 2, rows(w_out, (FIRST_KC[kc] if n == 0 else kc) * NC, n * NC), KC)
                if c >= C_OUT + 6 and c < C_OUT + 10:
                    q = c - C_OUT - 6
                    if q == 0:
                        sp.wait_ge(rstd_ready, 2)
                        sp.dma_start(gain1[:, :], g_post_mix.partition_broadcast(P)).then_inc(gain1_loaded, 16)
                    sp.dma_start(resid[:, q, :], x_rows[:, q, :]).then_inc(resid_loaded, 16)

            def load_in(half, off, w, i):
                for kc in range(KC):
                    load(half, off + kc, rows(w, kc * NC, i * NC), KC)

            def load_down(half, off, i):
                for n in range(NN):
                    load(half, off + n, rows(w_down, i * NC, n * NC), KC)

            load_in(C_FFN // 2, 0, w_gate, 0)
            load_in(C_FFN // 2, 4, w_up, 0)
            with sp.Fori(1, GROUPS) as i:
                half = C_FFN // 2 - 2 + 6 * i
                load_in(half, 0, w_gate, i)
                load_down(half, 4, i - 1)
                load_in(half, 8, w_up, i)
            load_down((C_LAST - 4) // 2, 0, GROUPS - 1)
            sp.wait_ge(h_lo_ready, KC * GROUPS)
            sp.dma_start(gain3[:, :], g_post_ffn.partition_broadcast(P)).then_inc(gain3_loaded, 16)
            for tb in range(TB):
                for n, cols in enumerate(HALVES):
                    sp.wait_ge(final_ready[tb], n + 1)
                    sp.dma_start(out[tb * P:(tb + 1) * P, cols], mixed[:, tb, cols]).then_inc(stored, 16)
            sp.wait_ge(stored, 16 * TB * len(HALVES))

        @block.tensor
        def _(pe):
            def products(ps, lhs, rhs, start, stop, shared=False):
                (lh, ll), (rh, rl) = lhs, rhs
                pe.matmul(ps, lh, rh, start=start, stop=False, skip_group_check=shared)
                pe.matmul(ps, lh, rl, start=False, stop=False, skip_group_check=shared)
                return pe.matmul(ps, ll, rh, start=False, stop=stop, skip_group_check=shared)

            def column_tile(half, off, ps, first=False, kts=range(KT), halfway=None):
                pe.wait_ge(split_ready, 2 * half + off + 1)
                for kt in kts:
                    if kt == KT // 2 and halfway is not None:
                        halfway()
                    if first:
                        pe.wait_ge(turned_lo, max(kt, 8) + 1)
                    cols = slice(kt * P, (kt + 1) * P)
                    mm = products(ps, (w_hi[:, off % 2, cols], w_lo[:, off % 2, cols]),
                                  (act_hi[:, kt, :], act_lo[:, kt, :]), kt == 0, kt == KT - 1)
                if kts[-1] == KT - 1:
                    mm.then_inc(chunk_used, 1)

            def turn(source, kt, bnk):
                for tb in range(TB):
                    mm = pe.transpose(bnk[:, tb * P:(tb + 1) * P], source[:, tb, kt * P:(kt + 1) * P],
                                      ident[:, :])
                mm.then_inc(turned, 1)

            pe.wait_ge(consts_ready, 1)
            for kt in range(KT):
                if kt % 4 == 0:
                    pe.wait_ge(x_loaded[kt // 4], 16)
                if kt >= 8:
                    pe.wait_ge(turned_lo, kt - 7)
                if kt == 12:
                    column_tile(0, 0, bank[0], True, range(KT // 2))
                turn(x_in, kt, bank[kt % 8])

            def across(n, diag, bnk):
                pe.wait_ge(diag_ready, n + 1)
                pe.matmul(bnk, ones[:, :], diag[:, :, :].rearrange("p t n -> p (t n)"),
                          start=True, stop=True).then_inc(row_sums, 1)

            def diag(t, b):
                return t[:, b * P:(b + 1) * P]

            def scores(h):
                pe.wait_ge(q_ready, h + 1)
                pe.wait_ge(k_ready, h + 1)
                for b, (o, n) in ROW.items():
                    mm = products(z_all[:, o:o + n], (diag(k_hi, b), diag(k_lo, b)),
                                  (q_hi[:, SEQ - n:SEQ], q_lo[:, SEQ - n:SEQ]), b < 3, False, True)
                mm.then_inc(scores_ready, 1)

            def turn_v(h):
                pe.wait_ge(v_out, h + 1)
                if not (isinstance(h, int) and h == 0):
                    pe.wait_ge(ya_ready, h)
                for b in range(TB):
                    mm = pe.transpose(diag(bank[6], b), diag(vT, b), ident[:, :])
                mm.then_inc(v_turned, 1)

            def suffix(h):
                pe.wait_ge(stick_ready, h + 1)
                for kb, (o, n) in ROW.items():
                    for jb in range(kb, TB):
                        at, m = ROW[jb]
                        for part in (soft_hi, soft_lo):
                            mm = pe.matmul(z_all[:, o + n - m:o + n], (tri_neg if jb == kb else ones_neg)[:, :],
                                           part[:, at:at + m], start=False, stop=part is soft_lo,
                                           skip_group_check=True)
                mm.then_inc(logw_ready, 1)

            def attend(h):
                pe.wait_ge(v_ready, h + 1)
                pe.wait_ge(weight_lo_ready, h + 1)
                for b, (o, n) in ROW.items():
                    mm = products(bank[6][:, SEQ - n:SEQ], (diag(v_hi, b), diag(v_lo, b)),
                                  (soft_hi[:, o:o + n], soft_lo[:, o:o + n]), b == 0, b == TB - 1, True)
                mm.then_inc(av_ready, 1)

            def gates(h, turn_no, slot, banks=GATE_BANKS):
                pe.wait_ge(xc_ready, h + 1)
                pe.wait_ge(gate_w_loaded[slot], 32 * turn_no)
                for n in range(2):
                    mm = pe.matmul(bank[banks[n]], gate_w[:, slot, n, :], xc[:, :], start=True, stop=True)
                mm.then_inc(gates_ready, 1)

            def head_of(half, h0, t, u, last=False):
                h, off = h0 + u, 5 * u
                first = isinstance(h, int) and h == 0
                if not first:
                    pe.wait_ge(x_out, h)
                column_tile(half, off + 1, bank[1],
                            halfway=(lambda: across(0, diag0, bank[7])) if first else None)
                pe.wait_ge(q_out, h + 1)
                column_tile(half, off + 2, bank[0])
                if not first:
                    pe.wait_ge(ri_ready, 2 * h)
                scores(h)
                pe.wait_ge(k_out, h + 1)
                column_tile(half, off + 3, bank[1])
                turn_v(h)
                if not first:
                    pe.wait_ge(g_out, h)
                column_tile(half, off + 4, bank[2])
                if last:
                    pe.wait_ge(x_out, h + 1)
                    gates(h, t + 1, u, LAST_GATE_BANKS)
                suffix(h)
                if not last:
                    pe.wait_ge(v_out, h + 1)
                    column_tile(half, off + 5, bank[0])
                    attend(h)
                    gates(h, t + 1, u)

            column_tile(0, 0, bank[0], True, range(KT // 2, KT))
            pe.wait_ge(consts_ready, 2)
            head_of(0, 0, 0, 0)
            head_of(0, 0, 0, 1)
            with pe.Fori(1, HEADS // 2 - 1) as t:
                head_of(5 * t, 2 * t, t, 0)
                head_of(5 * t, 2 * t, t, 1)
            t = HEADS // 2 - 1
            head_of(5 * t, 2 * t, t, 0)
            head_of(5 * t, 2 * t, t, 1, True)

            def row_blocks(half, off, lhs, k0, banks, start, stop, free=None, inputs=None, sem_each=None,
                           tbs=range(TB)):
                pe.wait_ge(split_ready, 2 * half + off + 1)
                for tb in tbs:
                    if free is not None:
                        free(tb)
                    for k in range(KC):
                        if inputs is not None and tb == 0:
                            inputs(k)
                        toks = slice(tb * P, (tb + 1) * P)
                        cols = slice(k * NC, (k + 1) * NC)
                        mm = products(banks[tb], (lhs[0][:, k0 + k, toks], lhs[1][:, k0 + k, toks]),
                                      (w_hi[:, off % 2, cols], w_lo[:, off % 2, cols]),
                                      start and k == 0, stop and k == KC - 1)
                    if sem_each is not None:
                        mm.then_inc(sem_each, 1)
                if sem_each is None:
                    mm.then_inc(chunk_used, 1)

            def token_sums(which, bnk):
                pe.wait_ge(ssq_made, which + 1)
                for tb in range(TB):
                    mm = pe.matmul(bnk[:, tb:tb + 1], ssq[:, which, tb * P:(tb + 1) * P], ones[:, 0:1],
                                   start=(tb == 0), stop=(tb == TB - 1), skip_group_check=True)
                mm.then_inc(ssq_ready, 1)

            def free_first(tb, c):
                if c == 0:
                    if tb == 1:
                        pe.wait_ge(ri_ready, 2 * HEADS)
                    if tb == 2:
                        pe.wait_ge(g_out, HEADS)
                elif c == 1:
                    if tb == 3:
                        pe.wait_ge(ya_ready, HEADS)
                        token_sums(0, bank[6])
                        pe.wait_ge(mean_ready, 2)
                elif c == KC:
                    pe.wait_ge(mix_a, tb + 1)
                    if tb == 3:
                        token_sums(1, bank[7])
                        pe.wait_ge(mean_ready, 3)

            for n in range(NN):
                for j in range(KC):
                    c = C_OUT + KC * n + j
                    kc = FIRST_KC[j] if n == 0 else j

                    def free(tb, n=n, kc=kc, c=c):
                        if c - C_OUT in (0, 1, KC):
                            free_first(tb, c - C_OUT)
                        elif kc % 2 == 0:
                            pe.wait_ge(mix_a if kc == 0 else mix_b, TB * (n - 1) + tb + 1)

                    def inputs(k, n=n, j=j):
                        if n == 0:
                            pe.wait_ge(y_lo, KC * j + k + 1)
                    row_blocks(c // 2, c % 2, (act_hi, act_lo), KC * kc, SET_A if kc < 2 else SET_B,
                               kc % 2 == 0, kc % 2 == 1, free, inputs, last_out if c == C_FFN - 1 else None)
                    if j == 0 and n == 0:
                        attend(HEADS - 1)

            def into_ffn(half, off, banks, kcs, early=False, inputs=None, halfway=None):
                for kc in kcs:
                    pe.wait_ge(split_ready, 2 * half + off + kc + 1)
                    slot = (off + kc) % 2
                    for f in range(KC):
                        if f == KC // 2 and halfway is not None:
                            halfway()
                        for k in range(KC):
                            if f == 0 and inputs is not None:
                                inputs(k)
                            at = k * NC + f * P
                            mm = products(banks[f], (w_hi[:, slot, at:at + P], w_lo[:, slot, at:at + P]),
                                          (act_hi[:, KC * kc + k, :], act_lo[:, KC * kc + k, :]),
                                          kc == k == 0, kc == k == KC - 1)
                        if early and kc == KC - 1 and f < KC - 1:
                            mm.then_inc(early_tile, 1)
                    mm.then_inc(chunk_used, 1)

            def turn_quarter(q):
                for k in range(4):
                    kt = 4 * q + k
                    pe.wait_ge(resid_ready, TB * (q + 1))
                    if q >= 1:
                        pe.wait_ge(turned_lo, KT + kt - 3)
                    turn(resid, kt, SET_B[k])

            F = C_FFN // 2
            for tb in range(TB):
                pe.wait_ge(resid_ready, tb + 1)
                for k in range(4):
                    if k == 3 and tb == 0:
                        pe.wait_ge(mix_b, TB * NN)
                    mm = pe.transpose(SET_B[k][:, tb * P:(tb + 1) * P], resid[:, tb, k * P:(k + 1) * P],
                                      ident[:, :])
                    if tb == TB - 1:
                        mm.then_inc(turned, 1)
            pe.wait_ge(mix_a, TB * NN)
            into_ffn(F, 0, SET_A, [0], inputs=lambda k: pe.wait_ge(turned_lo, KT + k + 1))
            for kc in range(1, KC):
                turn_quarter(kc)
                into_ffn(F, 0, SET_A, [kc], inputs=lambda k, kc=kc: pe.wait_ge(turned_lo, KT + KC * kc + k + 1),
                         halfway=(lambda: across(1, diag2, SET_B[0])) if kc == KC - 1 else None)
            pe.wait_ge(row_scale_ready, 1)
            into_ffn(F, 4, SET_B, range(KC), True)

            def down(half, off, i, sets, free, parts=NN):
                for n in range(parts):
                    free(n)
                    row_blocks(half, off + n, (h_hi, h_lo), 0, sets[n], True, True,
                               inputs=(lambda k: pe.wait_ge(h_lo_ready, KC * i + k + 1)) if n == 0 else None)

            def group(half, i, first=False):
                if first:
                    pe.wait_ge(gate_scaled, KC)
                else:
                    pe.wait_ge(down_out, TB * NN * (i - 1))
                into_ffn(half, 0, SET_A, range(KC))

                def free(n):
                    if n == 0:
                        pe.wait_ge(h_made, KC * i)
                    if n == 1:
                        pe.wait_ge(gate_scaled, KC * (i + 1))
                    if n >= 2:
                        pe.wait_ge(down_out, TB * NN * (i - 1) + TB * (n - 1))
                down(half, 4, i - 1, BABA, free)
                pe.wait_ge(down_out, TB * NN * (i - 1) + TB * 3)
                into_ffn(half, 8, SET_B, range(KC), True)

            group(F + 4, 1, True)
            with pe.Fori(2, GROUPS) as i:
                group(F - 2 + 6 * i, i)

            def free(n):
                if n == 0:
                    pe.wait_ge(down_out, TB * NN * (GROUPS - 1))
                if n == 1:
                    pe.wait_ge(h_made, KC * GROUPS)
                if n >= 2:
                    pe.wait_ge(down_out, TB * NN * (GROUPS - 1) + TB * (n - 1))
            down((C_LAST - 4) // 2, 0, GROUPS - 1, ABAB, free, NN - 2)
            for n, tb in LAST_BLOCKS:
                free(n)
                row_blocks((C_LAST - 4) // 2, n, (h_hi, h_lo), 0, ABAB[n], True, True, sem_each=last_out,
                           tbs=[tb])

        def until_used(engine, half, off, after_w_out=False):
            if isinstance(half, int):
                c = 2 * half + off
                if c == C_FFN - 1:
                    engine.wait_ge(last_out, TB)
                else:
                    engine.wait_ge(chunk_used, c + 1 - (c >= C_FFN))
            else:
                engine.wait_ge(chunk_used, 2 * half + off + (0 if after_w_out else 1))

        def y_source(ft):
            return gelu_t[:, :] if ft == KT - 1 else y_raw[:, ft, :]

        @block.scalar
        def _(act):
            step = Steps(act, act_steps)

            def high(half, off, kc=None, in_ffn=False):
                act.wait_ge(raw_loaded[off % 2], 16 * (half + off // 2 + 1))
                if not (isinstance(half, int) and 2 * half + off < 2):
                    until_used(act, half, off - 2, in_ffn)
                if kc is None:
                    nc.scalar.activation(w_hi[:, off % 2, :], w_raw[:, off % 2, :], ACT.Copy)\
                        .then_inc(hi_ready, 1)
                    return
                for k in range(KC):
                    cols, row = slice(k * NC, (k + 1) * NC), KC * kc + k
                    ins = nc.scalar.activation(w_hi[:, off % 2, cols], w_raw[:, off % 2, cols], ACT.Copy,
                                               scale=ffn_gain[:, row:row + 1])
                ins.then_inc(hi_ready, 1)

            def copy_high(dst, src, done, **scale):
                nc.scalar.activation(dst, src, ACT.Copy, **scale).then_inc(done, 1)

            def take_root(n):
                act.wait_ge(mean_ready, n)
                nc.scalar.activation(root, mean_sq, ACT.Sqrt).then_inc(root_ready, 1)

            act.wait_ge(gains_loaded, 32)
            lam = prm_all[:, :, PARAMS - 1]
            pos, neg = prm_all[:, :, PARAMS], prm_all[:, :, PARAMS + 1]
            step(nc.scalar.activation(pos, lam, ACT.Abs))
            step(nc.scalar.activation(pos, pos, ACT.Exp, scale=-1.0))
            step(nc.scalar.activation(pos, pos, ACT.Ln, bias=1.0))
            nc.scalar.activation(neg, lam, ACT.Relu, scale=-1.0).then_inc(coef_ready, 1)
            def square_input(q):
                for tb in range(2):
                    step(nc.scalar.activation(square0[:, 0, :], x_in[:, tb, q * NC:(q + 1) * NC], ACT.Square,
                                              accum_out=sums[:, tb, q:q + 1]))

            for kt in range(KT):
                act.wait_ge(turned, kt + 1)
                copy_high(act_hi[:, kt, :], bank[kt % 8], turned_hi, scale=in_gain[:, kt:kt + 1])
                if kt == 7:
                    high(0, 0)
                if kt == 11:
                    for q in range(3):
                        square_input(q)
            high(0, 1)
            square_input(3)
            take_root(1)
            act.wait_ge(consts_ready, 2)
            copy_high(tri_neg[:, :], made[:, 0, :], coef_ready)
            copy_high(ones_neg[:, :], made[:, 1, :], coef_ready)

            def q_high(h):
                if not (isinstance(h, int) and h == 0):
                    act.wait_ge(scores_ready, h)
                act.wait_ge(q_out, h + 1)
                copy_high(q_hi[:, :], qk_t[:, :], q_hi_ready)

            def y_high(n):
                ft = Y_ORDER[n]
                if ft == KT - 1:
                    act.wait_ge(yl_ready, HEADS)
                else:
                    act.wait_ge(ya_stored if ft < HEADS else yl_stored, ft % HEADS + 1)
                copy_high(act_hi[:, ft, :], y_source(ft), y_hi, scale=y_gain[:, ft:ft + 1])

            def gate_values(h, u, banks=GATE_BANKS):
                act.wait_ge(gates_ready, h + 1)
                act.wait_ge(params_ready, h + 1)
                nc.scalar.activation(r_t[:, :], bank[banks[0]], ACT.Sigmoid, bias=prm[:, u, 5:6])\
                    .then_inc(ri_ready, 1)
                nc.scalar.activation(i_t[:, :], bank[banks[1]], ACT.Sigmoid, bias=prm[:, u, 6:7])\
                    .then_inc(ri_ready, 1)

            def decay(h, u, last):
                act.wait_ge(ri_ready, 2 * h + 2)
                nc.scalar.activation(u_t[:, :], r_t[:, :], ACT.Tanh, scale=prm[:, u, 8:9]).then_inc(ua_ready, 1)
                nc.scalar.activation(a_t[:, :], r_t[:, :], ACT.Exp, scale=prm[:, u, 9:10]).then_inc(ua_ready, 1)
                if last:
                    high(C_OUT // 2 + 1, 1)
                act.wait_ge(v2_ready, h + 1)
                nc.scalar.activation(d_t[:, :], d_t[:, :], ACT.Sqrt).then_inc(mult_ready, 1)

            PER_HEAD = 2

            def head_of(half, h0, u, last=False):
                h, off = h0 + u, 5 * u
                first = isinstance(h, int) and h == 0
                high(half, off + 3)
                act.wait_ge(k_out, h + 1)
                if not first:
                    act.wait_ge(scores_ready, h)
                copy_high(k_hi[:, :], qk_t[:, :], k_hi_ready)
                high(half, off + 4)
                act.wait_ge(scores_ready, h + 1)
                if not first:
                    act.wait_ge(weight_lo_ready, h)
                step(nc.scalar.activation(soft[:, :], z_all[:, 0:SC], ACT.Abs))
                step(nc.scalar.activation(soft[:, :], soft[:, :], ACT.Exp, scale=-1.0))
                nc.scalar.activation(soft[:, :], soft[:, :], ACT.Ln, bias=1.0).then_inc(smooth_ready, 1)
                act.wait_ge(v_turned, h + 1)
                if not first:
                    act.wait_ge(av_ready, h)
                copy_high(v_hi[:, :], bank[6], v_hi_ready)
                high(half, off + 5)
                act.wait_ge(soft_ready, h + 1)
                copy_high(soft_hi[:, :], soft[:, :], stick_hi_ready)
                if last:
                    until_used(act, half, off + 4)
                    for n in range(KC):
                        y_high(n)
                    gate_values(h, u, LAST_GATE_BANKS)
                high(half, off + 6)
                act.wait_ge(logd_ready, h + 1)
                nc.scalar.activation(soft[:, :], z_all[:, 0:SC], ACT.Exp).then_inc(weight_ready, 1)
                act.wait_ge(weight_ready, h + 1)
                copy_high(soft_hi[:, :], soft[:, :], weight_hi_ready)
                act.wait_ge(g_out, h + 1)
                nc.scalar.activation(gelu_t[:, :], gelu_t[:, :], ACT.Gelu_apprx_tanh).then_inc(gelu_ready, 1)
                if not last:
                    high(half, off + 7)
                    q_high(h + 1)
                    gate_values(h, u)
                else:
                    for n in range(KC, 2 * KC):
                        y_high(n)
                    high(half, off + 7)
                    for n in range(2 * KC, 3 * KC):
                        y_high(n)
                decay(h, u, last)

            q_high(0)
            high(0, 2)
            head_of(0, 0, 0)
            head_of(0, 0, 1)
            with act.Fori(1, HEADS // 2 - 1) as t:
                step.loop(t, 1, 2 * PER_HEAD)
                head_of(5 * t, 2 * t, 0)
                head_of(5 * t, 2 * t, 1)
            step.end(HEADS // 2 - 2, 2 * PER_HEAD)
            t = HEADS // 2 - 1
            head_of(5 * t, 2 * t, 0)
            head_of(5 * t, 2 * t, 1, True)

            def half_roots(which):
                act.wait_ge(mean_ready, which + 2)
                nc.scalar.activation(half_root[which], half_mean[which], ACT.Sqrt).then_inc(root_ready, 1)

            def square_of(tb, n, made_before, done, source=None):
                act.wait_ge(*made_before)
                if done > 0:
                    act.wait_ge(mixed_squared, done)
                if source is None:
                    source = mixed[:, tb, n * NC:(n + 1) * NC]
                nc.scalar.activation(square[:, :], source, ACT.Square,
                                     accum_out=sums[:, tb, n:n + 1]).then_inc(mixed_squared, 1)

            def root_of(tb, count):
                act.wait_ge(mixed_squared, count)
                nc.scalar.activation(root[:, tb:tb + 1], sums[:, tb, NN - 1:NN], ACT.Sqrt, scale=1.0 / D,
                                     bias=mean_sq[:, tb:tb + 1]).then_inc(root_ready, 1)

            half_roots(0)
            for n in range(3 * KC, 4 * KC):
                y_high(n)
            F = C_FFN // 2
            for c in range(C_OUT + 2, C_FFN):
                n, j = divmod(c - C_OUT, KC)
                if c > C_OUT + 2:
                    high((c + 1) // 2, (c + 1) % 2, 0 if c + 1 == C_FFN else None)
                if j == (3 if n == 0 else 2):
                    until_used(act, (c - 1) // 2, (c - 1) % 2)
                    act.wait_ge(rstd_ready, 1)
                    act.wait_ge(y_lo, KT)
                    for tb in range(TB):
                        nc.scalar.activation(mixed[:, tb, n * NC:(n + 1) * NC], SET_A[tb], ACT.Copy,
                                             scale=half_rstd[0][:, tb:tb + 1]).then_inc(mix_a, 1)
                if n == 1 and j == 0:
                    half_roots(1)
                if n >= 1 and j == 1:
                    for tb in range(TB):
                        square_of(tb, n - 1, (mix_b, TB * (n - 1) + tb + 1), TB * (n - 1) + tb)
            act.wait_ge(mean_ready, 4)
            for tb in range(TB):
                square_of(tb, NN - 1, (mix_b, TB * (NN - 1) + tb + 1), TB * (NN - 1) + tb)
                root_of(tb, TB * (NN - 1) + tb + 1)
            def turned_high(q):
                for kt in range(4 * q, 4 * q + 4):
                    act.wait_ge(turned, KT + kt + 1)
                    copy_high(act_hi[:, kt, :], SET_B[kt % 4], turned_hi)

            def square_resid(tb):
                nc.scalar.activation(mixed[:, tb, :], resid[:, tb, :], ACT.Square,
                                     accum_out=total[:, tb:tb + 1]).then_inc(squared, 1)

            turned_high(0)
            high(F, 1, 1)
            turned_high(1)
            high(F, 2, 2)
            act.wait_ge(resid_ready, TB * 4)
            for tb in range(TB - 1):
                square_resid(tb)
            turned_high(2)
            square_resid(TB - 1)
            take_root(5)
            high(F, 3, 3)
            turned_high(3)

            def silu(i):
                for f in range(KC):
                    act.wait_ge(gate_scaled, KC * i + f + 1)
                    nc.scalar.activation(h_raw[:, f, :], h_raw[:, f, :], ACT.Silu).then_inc(silu_ready, 1)

            def h_high(i):
                for f in range(KC):
                    act.wait_ge(h_made, KC * i + f + 1)
                    copy_high(h_hi[:, f, :], h_raw[:, f, :], h_hi_ready)

            high(F, 4, 0)
            high(F, 5, 1)
            silu(0)
            high(F, 6, 2)
            high(F, 7, 3)
            high(F, 8, 0)
            h_high(0)

            def group(half, i, last=False):
                for c in range(12):
                    nxt = c + 1
                    kc = nxt % 4 if nxt < 4 or nxt >= 8 else None
                    if nxt == 12:
                        kc = None if last else 0
                    high(half, nxt, kc, True)
                    if c == 4:
                        silu(i)
                h_high(i)

            with act.Fori(1, GROUPS - 1) as i:
                group(F - 2 + 6 * i, i)
            half = F - 2 + 6 * (GROUPS - 1)
            group(half, GROUPS - 1, True)
            before, done = TB * NN * (GROUPS - 1), TB * NN
            high(half, 13)
            for n in range(NN - 2):
                high(half, 14 + n)
                for tb in range(TB):
                    square_of(tb, n, (down_out, before + TB * n + tb + 1), done + TB * n + tb)
            before, done = before + TB * (NN - 2), done + TB * (NN - 2)
            for m, (n, tb) in enumerate(LAST_BLOCKS):
                square_of(tb, n, (down_out, before + m + 1), done + m, last_cols[:, tb, :] if n == NN - 1 else None)
                if n == NN - 1:
                    act.wait_ge(mean_ready, 6 + max(tb - 1, 0))
                    root_of(tb, done + m + 1)

        @block.vector
        def _(dve):
            step = Steps(dve, dve_steps)
            SUB = ALU.subtract

            def low(half, off, kc=None):
                dve.wait_ge(hi_ready, 2 * half + off + 1)
                s = off % 2
                if kc is None:
                    nc.vector.tensor_tensor(w_lo[:, s, :], w_raw[:, s, :], w_hi[:, s, :].bitcast(F32), SUB)\
                        .then_inc(split_ready, 1)
                    return
                for k in range(KC):
                    cols, row = slice(k * NC, (k + 1) * NC), KC * kc + k
                    ins = nc.vector.scalar_tensor_tensor(
                        out=w_lo[:, s, cols], in0=w_raw[:, s, cols], scalar=ffn_gain[:, row:row + 1],
                        in1=w_hi[:, s, cols].bitcast(F32), op0=ALU.mult, op1=SUB)
                ins.then_inc(split_ready, 1)

            def rest(dst, src, high_part, done):
                nc.vector.tensor_tensor(dst, src, high_part.bitcast(F32), SUB).then_inc(done, 1)

            def mean(dst, src, n):
                nc.vector.tensor_scalar(dst, src, 1.0 / n, EPS, ALU.mult, ALU.add).then_inc(mean_ready, 1)

            def diagonal(diag, n):
                dve.wait_ge(root_ready, n)
                step(nc.vector.reciprocal(rstd, root))
                for tb in range(TB):
                    ins = nc.vector.tensor_scalar(diag[:, tb, :], ident[:, :], rstd[:, tb:tb + 1], None,
                                                  ALU.mult)
                ins.then_inc(diag_ready, 1)

            def square_input(q):
                for tb in range(2, TB):
                    part = x_in[:, tb, q * NC:(q + 1) * NC]
                    step(nc.vector.tensor_tensor_reduce(out=square0[:, 1, :], in0=part, in1=part, scale=1.0,
                                                        scalar=0.0, op0=ALU.mult, op1=ALU.add,
                                                        accum_out=sums[:, tb, q:q + 1]))

            dve.wait_ge(consts_ready, 1)
            dve.wait_ge(gains_loaded, 32)
            for kt in range(KT):
                dve.wait_ge(turned_hi, kt + 1)
                nc.vector.scalar_tensor_tensor(out=act_lo[:, kt, :], in0=bank[kt % 8],
                                               scalar=in_gain[:, kt:kt + 1],
                                               in1=act_hi[:, kt, :].bitcast(F32),
                                               op0=ALU.mult, op1=SUB).then_inc(turned_lo, 1)
                if kt == 7:
                    low(0, 0)
                if kt == 11:
                    for q in range(3):
                        square_input(q)
            low(0, 1)
            square_input(3)
            dve.wait_ge(act_steps, 11)
            step(nc.vector.reduce_sum(total, sums, AX_X))
            mean(mean_sq, total, D)
            diagonal(diag0, 1)
            dve.wait_ge(row_sums, 1)
            step(nc.vector.tensor_copy(row_scale[:, :], bank[7]))

            def scaled_out(dst, bnk, done):
                nc.vector.tensor_tensor(dst, bnk, row_scale[:, :], ALU.mult).then_inc(done, 1)

            def q_scaled(half, off):
                until_used(dve, half, off)
                nc.vector.scalar_tensor_tensor(out=qk_t[:, :], in0=bank[0], scalar=SCALE,
                                               in1=row_scale[:, :], op0=ALU.mult, op1=ALU.mult)\
                    .then_inc(q_out, 1)

            def q_low(h):
                dve.wait_ge(q_hi_ready, h + 1)
                rest(q_lo[:, :], qk_t[:, :], q_hi[:, :], q_ready)

            def y_low(n):
                ft = Y_ORDER[n]
                dve.wait_ge(y_hi, n + 1)
                nc.vector.scalar_tensor_tensor(out=act_lo[:, ft, :], in0=y_source(ft),
                                               scalar=y_gain[:, ft:ft + 1],
                                               in1=act_hi[:, ft, :].bitcast(F32),
                                               op0=ALU.mult, op1=SUB).then_inc(y_lo, 1)

            def half_mean_of(which, bnk):
                dve.wait_ge(ssq_ready, which + 1)
                mean(half_mean[which], bnk[:, 0:TB], HALF)

            def half_scale(which):
                dve.wait_ge(root_ready, which + 2)
                nc.vector.reciprocal(half_rstd[which], half_root[which]).then_inc(rstd_ready, 1)

            q_scaled(0, 0)
            pos, neg = prm_all[:, :, PARAMS], prm_all[:, :, PARAMS + 1]
            dve.wait_ge(coef_ready, 1)
            step(nc.vector.tensor_tensor(pos, pos, neg, ALU.add))
            step(nc.vector.tensor_scalar(pos, pos, LRU_C, None, ALU.mult))
            nc.vector.tensor_scalar(neg, pos, -1.0, None, ALU.mult).then_inc(coef_ready, 1)
            step(nc.vector.memset(xs[:, 0:CONV - 1], 0.0))
            dve.wait_ge(consts_ready, 2)
            q_low(0)
            low(0, 2)
            PER_HEAD = 9

            def on_diagonal(t):
                return (t[:, 0:2 * NC].rearrange("p (b t) -> p b t", b=2)[:, :, 0:P],
                        t[:, ROW[3][0]:ROW[3][0] + 2 * P].rearrange("p (b t) -> p b t", b=2))

            later2, never2 = (t[:, :].unsqueeze(1).broadcast_to([P, 2, P]) for t in (later, never))

            def head_of(half, h0, u, last=False):
                h, off = h0 + u, 5 * u
                first = isinstance(h, int) and h == 0
                pr = prm[:, u, :]
                until_used(dve, half, off + 1)
                dve.wait_ge(q_ready, h + 1)
                scaled_out(qk_t[:, :], bank[1], k_out)
                low(half, off + 3)
                dve.wait_ge(k_hi_ready, h + 1)
                rest(k_lo[:, :], qk_t[:, :], k_hi[:, :], k_ready)
                until_used(dve, half, off + 2)
                if not first:
                    dve.wait_ge(v_turned, h)
                scaled_out(vT[:, :], bank[0], v_out)
                low(half, off + 4)
                dve.wait_ge(smooth_ready, h + 1)
                step(nc.vector.scalar_tensor_tensor(out=soft[:, :], in0=z_all[:, 0:SC], scalar=0.0,
                                                    in1=soft[:, :], op0=ALU.max, op1=ALU.add))
                for two in on_diagonal(soft):
                    ins = nc.vector.tensor_tensor(two, two, later2, ALU.mult)
                ins.then_inc(soft_ready, 1)
                dve.wait_ge(v_hi_ready, h + 1)
                rest(v_lo[:, :], bank[6], v_hi[:, :], v_ready)
                until_used(dve, half, off + 3)
                scaled_out(xs[:, CONV - 1:CONV - 1 + SEQ], bank[1], x_out)
                low(half, off + 5)
                dve.wait_ge(stick_hi_ready, h + 1)
                rest(soft_lo[:, :], soft[:, :], soft_hi[:, :], stick_ready)
                dve.wait_ge(x_out, h + 1)
                dve.wait_ge(params_ready, h + 1)
                step(nc.vector.tensor_scalar(xc[:, :], xs[:, 0:SEQ], pr[:, 0:1], pr[:, 4:5],
                                             ALU.mult, ALU.add))
                for k in range(1, CONV):
                    ins = nc.vector.scalar_tensor_tensor(out=xc[:, :], in0=xs[:, k:k + SEQ],
                                                         scalar=pr[:, k:k + 1], in1=xc[:, :],
                                                         op0=ALU.mult, op1=ALU.add)
                    if k < CONV - 1:
                        step(ins)
                    else:
                        ins.then_inc(xc_ready, 1)
                until_used(dve, half, off + 4)
                if not first:
                    dve.wait_ge(yl_stored, h)
                scaled_out(gelu_t[:, :], bank[2], g_out)
                if last:
                    for n in range(KC):
                        y_low(n)
                low(half, off + 6)
                dve.wait_ge(logw_ready, h + 1)
                for two in on_diagonal(z_all):
                    ins = nc.vector.tensor_tensor(two, two, never2, ALU.add)
                ins.then_inc(logd_ready, 1)
                dve.wait_ge(weight_hi_ready, h + 1)
                rest(soft_lo[:, :], soft[:, :], soft_hi[:, :], weight_lo_ready)
                if not last:
                    dve.wait_ge(k_ready, h + 1)
                    q_scaled(half, off + 5)
                    low(half, off + 7)
                    q_low(h + 1)
                else:
                    for n in range(KC, 2 * KC):
                        y_low(n)
                    low(half, off + 7)
                dve.wait_ge(av_ready, h + 1)
                if not first:
                    dve.wait_ge(ya_stored, h)
                nc.vector.tensor_copy(ya_t[:, :], bank[6]).then_inc(ya_ready, 1)
                if last:
                    half_mean_of(0, bank[6])
                    for n in range(2 * KC, 3 * KC):
                        y_low(n)
                dve.wait_ge(ua_ready, 2 * h + 2)
                step(nc.vector.tensor_scalar(d_t[:, :], u_t[:, :], 1.0, None, ALU.add))
                step(nc.vector.reciprocal(d_t[:, :], d_t[:, :]))
                nc.vector.scalar_tensor_tensor(out=d_t[:, :], in0=u_t[:, :], scalar=2.0, in1=d_t[:, :],
                                               op0=ALU.mult, op1=ALU.mult).then_inc(v2_ready, 1)
                step(nc.vector.tensor_tensor(i_t[:, :], i_t[:, :], xc[:, :], ALU.mult))
                dve.wait_ge(mult_ready, h + 1)
                step(nc.vector.tensor_tensor(i_t[:, :], i_t[:, :], d_t[:, :], ALU.mult))
                step(nc.vector.tensor_tensor_scan(u_t[:, :], a_t[:, :], i_t[:, :], 0.0, ALU.mult, ALU.add))
                dve.wait_ge(gelu_ready, h + 1)
                nc.vector.tensor_tensor(gelu_t[:, :], u_t[:, :], gelu_t[:, :], ALU.mult).then_inc(yl_ready, 1)

            head_of(0, 0, 0)
            head_of(0, 0, 1)
            with dve.Fori(1, HEADS // 2 - 1) as t:
                step.loop(t, 1, 2 * PER_HEAD)
                head_of(5 * t, 2 * t, 0)
                head_of(5 * t, 2 * t, 1)
            step.end(HEADS // 2 - 2, 2 * PER_HEAD)
            t = HEADS // 2 - 1
            head_of(5 * t, 2 * t, 0)
            head_of(5 * t, 2 * t, 1, True)

            def mean_but_last(count, tbs=slice(0, TB)):
                dve.wait_ge(mixed_squared, count)
                step(nc.vector.reduce_sum(total[:, tbs], sums[:, tbs, 0:NN - 1], AX_X))
                mean(mean_sq[:, tbs], total[:, tbs], D)

            def add_lru(n, tb):
                cols = slice(n * NC, (n + 1) * NC)
                dve.wait_ge(mix_a, TB * n + tb + 1)
                nc.vector.scalar_tensor_tensor(out=mixed[:, tb, cols], in0=SET_B[tb],
                                               scalar=half_rstd[1][:, tb:tb + 1], in1=mixed[:, tb, cols],
                                               op0=ALU.mult, op1=ALU.add).then_inc(mix_b, 1)

            half_scale(0)
            low(C_OUT // 2 + 1, 1)
            for n in range(3 * KC, 4 * KC):
                y_low(n)
            F = C_FFN // 2
            for c in range(C_OUT + 2, C_FFN):
                n, j = divmod(c - C_OUT, KC)
                if c > C_OUT + 2:
                    low((c + 1) // 2, (c + 1) % 2, 0 if c + 1 == C_FFN else None)
                if n == 1 and j == 0:
                    half_mean_of(1, bank[7])
                    half_scale(1)
                    dve.wait_ge(rstd_ready, 2)
                if n >= 1 and j == 0:
                    until_used(dve, (c - 1) // 2, (c - 1) % 2)
                    for tb in range(TB):
                        add_lru(n - 1, tb)
                if c == C_FFN - 2:
                    mean_but_last(TB * (NN - 1))
            def part_rstd(tbs):
                dve.wait_ge(root_ready, 3 + tbs.stop)
                step(nc.vector.reciprocal(rstd[:, tbs], root[:, tbs]))

            def add_mixed(q, tbs=range(TB)):
                cols = slice(q * NC, (q + 1) * NC)
                dve.wait_ge(mixed_scaled, TB * (q + 1))
                for tb in tbs:
                    nc.vector.scalar_tensor_tensor(out=resid[:, tb, cols], in0=mixed[:, tb, cols],
                                                   scalar=rstd[:, tb:tb + 1], in1=resid[:, tb, cols],
                                                   op0=ALU.mult, op1=ALU.add).then_inc(resid_ready, 1)

            dve.wait_ge(resid_loaded, 16 * TB)
            for tb in range(TB):
                dve.wait_ge(last_out, tb + 1)
                add_lru(NN - 1, tb)
                if tb == 2:
                    part_rstd(slice(0, 2))
                    add_mixed(0, range(2))
            part_rstd(slice(2, 4))
            add_mixed(0, range(2, TB))

            def turned_rest(q):
                for kt in range(4 * q, 4 * q + 4):
                    dve.wait_ge(turned_hi, KT + kt + 1)
                    rest(act_lo[:, kt, :], SET_B[kt % 4], act_hi[:, kt, :], turned_lo)

            turned_rest(0)
            add_mixed(1)
            low(F, 1, 1)
            add_mixed(2)
            turned_rest(1)
            add_mixed(3)
            low(F, 2, 2)
            turned_rest(2)
            dve.wait_ge(squared, TB)
            mean(mean_sq, total, D)
            diagonal(diag2, 8)
            low(F, 3, 3)
            turned_rest(3)
            dve.wait_ge(row_sums, 2)
            nc.vector.tensor_copy(row_scale2[:, :], SET_B[0]).then_inc(row_scale_ready, 1)

            def gate_out(i, half, off):
                until_used(dve, half, off, True)
                for f in range(KC):
                    nc.vector.tensor_tensor(h_raw[:, f, :], SET_A[f], row_scale2[:, :], ALU.mult)\
                        .then_inc(gate_scaled, 1)

            def h_make(i, half, off):
                dve.wait_ge(silu_scaled, KC * (i + 1))
                for f in range(KC):
                    if f < KC - 1:
                        dve.wait_ge(early_tile, (KC - 1) * i + f + 1)
                    else:
                        until_used(dve, half, off, True)
                    nc.vector.tensor_tensor(h_raw[:, f, :], SET_B[f], h_raw[:, f, :], ALU.mult)\
                        .then_inc(h_made, 1)
                    dve.wait_ge(h_hi_ready, KC * i + f + 1)
                    rest(h_lo[:, f, :], h_raw[:, f, :], h_hi[:, f, :], h_lo_ready)

            def add_down(half, off, n, banks, first=False):
                until_used(dve, half, off, True)
                for tb in range(TB):
                    to = mixed[:, tb, n * NC:(n + 1) * NC]
                    if first:
                        nc.vector.tensor_copy(to, banks[tb]).then_inc(down_out, 1)
                    else:
                        nc.vector.tensor_tensor(to, banks[tb], to, ALU.add).then_inc(down_out, 1)

            low(F, 4, 0)
            dve.wait_ge(row_scale_ready, 1)
            gate_out(0, F, 3)
            low(F, 5, 1)
            low(F, 6, 2)
            low(F, 7, 3)
            low(F, 8, 0)
            h_make(0, F, 7)

            def group(half, i, first=False, last=False):
                for c in range(12):
                    nxt = c + 1
                    kc = nxt % 4 if nxt < 4 or nxt >= 8 else None
                    if nxt == 12:
                        kc = None if last else 0
                    if c == 4:
                        gate_out(i, half, 3)
                    low(half, nxt, kc)
                    if 5 <= c <= 8:
                        add_down(half, c - 1, c - 5, BABA[c - 5], first)
                h_make(i, half, 11)

            group(F + 4, 1, True)
            with dve.Fori(2, GROUPS - 1) as i:
                group(F - 2 + 6 * i, i)
            half = F - 2 + 6 * (GROUPS - 1)
            group(half, GROUPS - 1, False, True)
            for n in range(NN - 2):
                low(half, 13 + n)
                add_down(half, 12 + n, n, ABAB[n])
            low(half, 13 + NN - 2)

            def last_sum(n, tb):
                dve.wait_ge(last_out, TB + LAST_BLOCKS.index((n, tb)) + 1)
                old = mixed[:, tb, n * NC:(n + 1) * NC]
                nc.vector.tensor_tensor(last_cols[:, tb, :] if n == NN - 1 else old, ABAB[n][tb], old, ALU.add)\
                    .then_inc(down_out, 1)

            def last_rstd(tb):
                dve.wait_ge(root_ready, 9 + tb)
                nc.vector.reciprocal(rstd[:, tb:tb + 1], root[:, tb:tb + 1]).then_inc(rstd_ready, 1)

            def add_resid(tb, parts=HALVES):
                dve.wait_ge(rstd_ready, 3 + tb)
                dve.wait_ge(last_scaled, tb + 1)
                for cols in parts:
                    nc.vector.scalar_tensor_tensor(out=mixed[:, tb, cols], in0=mixed[:, tb, cols],
                                                   scalar=rstd[:, tb:tb + 1], in1=resid[:, tb, cols],
                                                   op0=ALU.mult, op1=ALU.add).then_inc(final_ready[tb], 1)

            squares = TB * NN + TB * (NN - 2)
            last_sum(2, 0)
            last_sum(2, 1)
            mean_but_last(squares + 2, slice(0, 2))
            last_sum(3, 0)
            last_sum(3, 1)
            last_rstd(0)
            add_resid(0)
            last_sum(2, 2)
            last_rstd(1)
            mean_but_last(squares + 5, slice(2, 3))
            add_resid(1)
            last_sum(3, 2)
            last_sum(2, 3)
            last_rstd(2)
            add_resid(2, HALVES[:1])
            mean_but_last(squares + 7, slice(3, 4))
            last_sum(3, 3)
            add_resid(2, HALVES[1:])
            last_rstd(3)
            add_resid(3)

        @block.gpsimd
        def _(pool):
            step = Steps(pool, pool_steps)
            step(nc.gpsimd.memset(ident[:, :], 0.0))
            step(nc.gpsimd.memset(ones[:, :], 1.0))
            nc.gpsimd.affine_select(out=ident[:, :], in_=ident[:, :], compare_op=ALU.not_equal, fill=1.0,
                                    base=0, pattern=[[-1, P]], channel_multiplier=1).then_inc(consts_ready, 1)
            step(nc.gpsimd.memset(made, -1.0))
            step(nc.gpsimd.memset(later[:, :], 1.0))
            step(nc.gpsimd.memset(never[:, :], 0.0))
            step(nc.gpsimd.affine_select(out=made[:, 0, :], in_=made[:, 0, :], compare_op=ALU.is_ge, fill=0.0,
                                         base=0, pattern=[[-1, P]], channel_multiplier=1))
            step(nc.gpsimd.affine_select(out=later[:, :], in_=later[:, :], compare_op=ALU.is_gt,
                                         fill=0.0, base=0, pattern=[[1, P]], channel_multiplier=-1))
            nc.gpsimd.affine_select(out=never[:, :], in_=never[:, :], compare_op=ALU.is_gt,
                                    fill=NEVER, base=0, pattern=[[1, P]], channel_multiplier=-1)\
                .then_inc(consts_ready, 1)
            pool.wait_ge(row_sums, 1)
            step(nc.gpsimd.memset(ssq[:, :, :], 0.0))
            pool.wait_ge(coef_ready, 4)

            def store(h, which, src, done, last):
                at = y_raw[:, bass.ds(h + HEADS * which, 1), :].rearrange("p a n -> p (a n)")
                step(nc.gpsimd.tensor_tensor(sq_t[:, :], src, src, ALU.mult))
                add = nc.gpsimd.tensor_tensor(ssq[:, which, :], ssq[:, which, :], sq_t[:, :], ALU.add)
                if last:
                    add.then_inc(ssq_made, 1)
                    pool.wait_ge(ssq_made, which + 1)
                else:
                    step(add)
                if not (last and which == 1):
                    nc.gpsimd.tensor_copy(at, src).then_inc(done, 1)

            def params(h, u):
                nc.gpsimd.tensor_copy(prm[:, u, :], prm_all[:, bass.ds(h, 1), :]
                                      .rearrange("p a n -> p (a n)")).then_inc(params_ready, 1)

            def head_of(h, u, more, last=False):
                pool.wait_ge(ya_ready, h + 1)
                store(h, 0, ya_t[:, :], ya_stored, last)
                pool.wait_ge(yl_ready, h + 1)
                store(h, 1, gelu_t[:, :], yl_stored, last)
                if more:
                    params(h + 2, u)

            params(0, 0)
            params(1, 1)
            with pool.Fori(0, HEADS // 2 - 1) as t:
                step.loop(t, 0, 8)
                head_of(2 * t, 0, True)
                head_of(2 * t + 1, 1, True)
            step.end(HEADS // 2 - 1, 8)
            head_of(HEADS - 2, 0, False)
            head_of(HEADS - 1, 1, False, True)

            def scale_parts(gain, before, parts):
                for n in range(parts):
                    for tb in range(TB):
                        cols = slice(n * NC, (n + 1) * NC)
                        pool.wait_ge(mixed_squared, before + TB * n + tb + 1)
                        nc.gpsimd.tensor_tensor(mixed[:, tb, cols], mixed[:, tb, cols], gain[:, cols],
                                                ALU.mult).then_inc(mixed_scaled, 1)

            pool.wait_ge(gain1_loaded, 16)
            scale_parts(gain1, 0, NN)
            pool.wait_ge(row_scale_ready, 1)

            def scale_silu(i):
                for f in range(KC):
                    pool.wait_ge(silu_ready, KC * i + f + 1)
                    nc.gpsimd.tensor_tensor(h_raw[:, f, :], h_raw[:, f, :], row_scale2[:, :], ALU.mult)\
                        .then_inc(silu_scaled, 1)

            with pool.Fori(0, GROUPS) as i:
                scale_silu(i)
            pool.wait_ge(gain3_loaded, 16)
            scale_parts(gain3, TB * NN, NN - 2)
            before, done = TB * NN * GROUPS - 2 * TB, 2 * TB * NN - 2 * TB
            for m, (n, tb) in enumerate(LAST_BLOCKS):
                cols = slice(n * NC, (n + 1) * NC)
                if n < NN - 1:
                    pool.wait_ge(mixed_squared, done + m + 1)
                    nc.gpsimd.tensor_tensor(mixed[:, tb, cols], mixed[:, tb, cols], gain3[:, cols], ALU.mult)\
                        .then_inc(mixed_scaled, 1)
                else:
                    pool.wait_ge(down_out, before + m + 1)
                    nc.gpsimd.tensor_tensor(mixed[:, tb, cols], last_cols[:, tb, :], gain3[:, cols], ALU.mult)\
                        .then_inc(last_scaled, 1)


def kernel(x, pre_mix_norm, post_mix_norm, pre_ffn_norm, post_ffn_norm, w_in, conv_w, conv_b,
           w_rgate, b_rgate, w_igate, b_igate, lru_lambda, attn_out_norm, lru_out_norm, w_out,
           w_ffn_gate, w_ffn_up, w_ffn_down):
    import numpy as np
    import concourse.bacc as bacc
    from concourse.bass_utils import run_bass_kernel_spmd

    a = {k: np.asarray(v) for k, v in locals().items() if k not in ("np", "bacc", "run_bass_kernel_spmd")}
    seq, d = a["x"].shape[1:]
    params = np.concatenate([a["conv_w"][0], a["conv_b"], a["b_rgate"], a["b_igate"], a["lru_lambda"]])
    col_gains = np.concatenate([a["pre_mix_norm"], a["attn_out_norm"], a["lru_out_norm"],
                                a["pre_ffn_norm"]], 1)
    arrays = {
        "x_in_dram": a["x"].reshape(seq, d),
        "col_gains": col_gains.reshape(3, d // P, P).transpose(2, 0, 1),
        "g_post_mix": a["post_mix_norm"].reshape(d),
        "g_post_ffn": a["post_ffn_norm"].reshape(d),
        "w_in_dram": a["w_in"][0],
        "lru_params": params.reshape(PARAMS, HEADS, P).transpose(2, 1, 0),
        "w_rgate_dram": a["w_rgate"][0],
        "w_igate_dram": a["w_igate"][0],
        "w_out_dram": a["w_out"][0],
        "w_gate_dram": a["w_ffn_gate"][0],
        "w_up_dram": a["w_ffn_up"][0],
        "w_down_dram": a["w_ffn_down"][0],
    }
    arrays = {k: np.ascontiguousarray(v) for k, v in arrays.items()}
    nc = bacc.Bacc("TRN2", target_bir_lowering=False, num_devices=1)
    args = [nc.dram_tensor(k, v.shape, mybir.dt.from_np(v.dtype), kind="ExternalInput").ap()
            for k, v in arrays.items()]
    args.append(nc.dram_tensor("out_dram", (seq, d), F32, kind="ExternalOutput").ap())
    decoder_layer(nc, *args)
    got = run_bass_kernel_spmd(nc, [arrays], core_ids=[0])
    return got.results[0]["out_dram"].reshape(1, seq, d)
```
